# Optimizing a Trainium2 kernel written in Bass

```python
import jax, jax.numpy as jnp
from jax import lax
import numpy as np
import math

D_MODEL = 1024
BATCH = 1
SEQ = 256
DEPTH = 2

N_EVEN = (DEPTH + 1) // 2
N_ODD = DEPTH // 2
EPS = 1e-6

GLA_HEADS = 4
GLA_DK = 64
GLA_DV = 128
GLA_RANK = 16
GLA_TAU = 16.0
GLA_CHUNK = 64
GLA_QK = GLA_HEADS * GLA_DK
GLA_V = GLA_HEADS * GLA_DV

SWA_HEADS = 8
SWA_KV_HEADS = 2
SWA_HEAD_DIM = 64
SWA_GROUP = SWA_HEADS // SWA_KV_HEADS
WINDOW = 128
SWA_BLOCK = 128
SWA_Q = SWA_HEADS * SWA_HEAD_DIM
SWA_KV = SWA_KV_HEADS * SWA_HEAD_DIM

N_BUCKETS = 32
MAX_DISTANCE = 128

IN_SPLITS = (GLA_QK, GLA_QK, GLA_V, GLA_V, GLA_RANK, SWA_Q, SWA_KV, SWA_KV)
IN_COLS = GLA_QK + GLA_QK + GLA_V + GLA_V + GLA_RANK + SWA_Q + SWA_KV + SWA_KV
MIX_OUT = GLA_V + SWA_Q

POOL_WINDOWS = (2, 4, 8, 16)
POOL_GROUP = D_MODEL // 4

D_FF = 4 * D_MODEL


def rms_norm(x, w):
    xf = x.astype(jnp.float32)
    y = xf * lax.rsqrt(jnp.mean(xf * xf, axis=-1, keepdims=True) + EPS)
    return (y * w.astype(jnp.float32)).astype(x.dtype)

def ada_modulation(c, w, b):
    mod = jax.nn.silu(c) @ w + b
    shift, scale, gate = jnp.split(mod, 3, axis=-1)
    return shift[:, None], scale[:, None], gate[:, None]

def t5_bucket(dist):
    max_exact = N_BUCKETS // 2
    d = np.maximum(dist, 1).astype(np.float64)
    large = max_exact + (np.log(d / max_exact) / np.log(MAX_DISTANCE / max_exact)
                         * (N_BUCKETS - max_exact)).astype(np.int32)
    large = np.minimum(large, N_BUCKETS - 1)
    return np.where(dist < max_exact, dist, large).astype(np.int32)

def gla_chunked(q, k, v, log_a):
    B, S, H, dk = q.shape
    dv = v.shape[-1]
    C = GLA_CHUNK
    nc = S // C
    f32 = jnp.float32
    qf = (q.astype(f32) * dk ** -0.5).reshape(B, nc, C, H, dk)
    kf = k.astype(f32).reshape(B, nc, C, H, dk)
    vf = v.astype(f32).reshape(B, nc, C, H, dv)
    b = jnp.cumsum(log_a.reshape(B, nc, C, H, dk), axis=2)
    b_last = b[:, :, -1]
    q_t = qf * jnp.exp(b)
    k_t = kf * jnp.exp(-b)
    k_end = kf * jnp.exp(b_last[:, :, None] - b)
    causal = jnp.tril(jnp.ones((C, C), dtype=bool))
    a = jnp.einsum('bnihd,bnjhd->bnhij', q_t, k_t)
    a = jnp.where(causal, a, 0.0)
    o_intra = jnp.einsum('bnhij,bnjhe->bnihe', a, vf)
    d_state = jnp.einsum('bnjhd,bnjhe->bnhde', k_end, vf)
    decay = jnp.exp(b_last)

    def step(s_prev, inp):
        ds, dec = inp
        return dec[..., None] * s_prev + ds, s_prev

    _, s_in = lax.scan(step, jnp.zeros((B, H, dk, dv), f32),
                       (jnp.moveaxis(d_state, 1, 0), jnp.moveaxis(decay, 1, 0)))
    s_in = jnp.moveaxis(s_in, 0, 1)
    o_inter = jnp.einsum('bnihd,bnhde->bnihe', q_t, s_in)
    return (o_intra + o_inter).reshape(B, S, H, dv)

def sliding_window_attention(q, k, v, rel_bias, sinks):
    B, S = q.shape[0], q.shape[1]
    nb = S // SWA_BLOCK
    L = SWA_BLOCK
    f32 = jnp.float32
    qb = q.reshape(B, nb, L, SWA_KV_HEADS, SWA_GROUP, SWA_HEAD_DIM)

    def band(t):
        tb = t.reshape(B, nb, L, SWA_KV_HEADS, SWA_HEAD_DIM)
        prev = jnp.pad(tb, ((0, 0), (1, 0), (0, 0), (0, 0), (0, 0)))[:, :-1]
        return jnp.concatenate([prev, tb], axis=2)

    kb, vb = band(k), band(v)
    s = jnp.einsum('bnqhgd,bnkhd->bnhgqk', qb, kb,
                   preferred_element_type=f32) * (SWA_HEAD_DIM ** -0.5)
    qi = np.arange(L)[:, None] + L
    kj = np.arange(2 * L)[None, :]
    dist = qi - kj
    valid = (dist >= 0) & (dist < WINDOW)
    bucket = t5_bucket(np.maximum(dist, 0))
    bias = jnp.transpose(rel_bias[jnp.asarray(bucket)].astype(f32), (2, 0, 1))
    s = s + bias.reshape(SWA_KV_HEADS, SWA_GROUP, L, 2 * L)
    blk_ok = (np.arange(nb)[:, None, None] > 0) | (np.arange(2 * L)[None, None, :] >= L)
    mask = valid[None] & blk_ok
    s = jnp.where(jnp.asarray(mask)[None, :, None, None], s, -1e30)
    sink = sinks.astype(f32).reshape(SWA_KV_HEADS, SWA_GROUP)[None, None, :, :, None, None]
    m = jnp.maximum(jnp.max(s, axis=-1, keepdims=True), sink)
    p = jnp.exp(s - m)
    p = p / (jnp.sum(p, axis=-1, keepdims=True) + jnp.exp(sink - m))
    o = jnp.einsum('bnhgqk,bnkhd->bnqhgd', p, vb.astype(f32))
    return o.reshape(B, S, SWA_Q).astype(q.dtype)

def hybrid_attention_mixer(h, w_in, gla_w_gate, gla_b_gate, gla_norm_w, sinks, rel_bias, w_out):
    B, S, _ = h.shape
    proj = h @ w_in
    offs = np.cumsum(IN_SPLITS)[:-1].tolist()
    gq, gk, gv, gg, glr, sq, sk, sv = jnp.split(proj, offs, axis=-1)
    gate_logits = (glr @ gla_w_gate + gla_b_gate).astype(jnp.float32)
    log_a = (jax.nn.log_sigmoid(gate_logits) / GLA_TAU).reshape(B, S, GLA_HEADS, GLA_DK)
    o_gla = gla_chunked(gq.reshape(B, S, GLA_HEADS, GLA_DK), gk.reshape(B, S, GLA_HEADS, GLA_DK),
                        gv.reshape(B, S, GLA_HEADS, GLA_DV), log_a).astype(h.dtype)
    o_gla = rms_norm(o_gla, gla_norm_w) * jax.nn.silu(gg.reshape(B, S, GLA_HEADS, GLA_DV))
    o_gla = o_gla.reshape(B, S, GLA_V)
    o_swa = sliding_window_attention(sq.reshape(B, S, SWA_HEADS, SWA_HEAD_DIM),
                                     sk.reshape(B, S, SWA_KV_HEADS, SWA_HEAD_DIM),
                                     sv.reshape(B, S, SWA_KV_HEADS, SWA_HEAD_DIM), rel_bias, sinks)
    return jnp.concatenate([o_gla, o_swa], axis=-1) @ w_out

def multiscale_pool_mixer(h, pool_w, pool_scale):
    B, S, _ = h.shape
    hf = h.astype(jnp.float32)
    cs = jnp.cumsum(hf, axis=1)
    t = jnp.arange(S)
    outs = []
    for gi, w in enumerate(POOL_WINDOWS):
        lo, hi = gi * POOL_GROUP, (gi + 1) * POOL_GROUP
        csg = cs[..., lo:hi]
        lag = jnp.pad(csg, ((0, 0), (w, 0), (0, 0)))[:, :S]
        cnt = jnp.minimum(t + 1, w).astype(jnp.float32)[None, :, None]
        pooled = (csg - lag) / cnt - hf[..., lo:hi]
        outs.append(pooled.astype(h.dtype) @ pool_w[gi])
    return jnp.concatenate(outs, axis=-1) * pool_scale

def squared_relu_mlp(h, w1, w2):
    return jnp.square(jax.nn.relu(h @ w1)) @ w2

def first_inputs(seed: int = 0) -> dict:
    key = jax.random.key(seed)
    ks = jax.random.split(key, 17)
    f32 = jnp.float32
    nrm = lambda k, s: jax.random.normal(k, s, f32)
    return {
        "x": nrm(ks[0], (BATCH, SEQ, D_MODEL)),
        "c": nrm(ks[1], (BATCH, D_MODEL)),
        "norm_w": 1.0 + 0.05 * nrm(ks[2], (DEPTH, 2, D_MODEL)),
        "ada_w": nrm(ks[3], (DEPTH, 2, D_MODEL, 3 * D_MODEL)) * (0.5 * D_MODEL ** -0.5),
        "ada_b": 0.01 * nrm(ks[4], (DEPTH, 2, 3 * D_MODEL)),
        "attn_w_in": nrm(ks[5], (N_EVEN, D_MODEL, IN_COLS)) * D_MODEL ** -0.5,
        "gla_w_gate": nrm(ks[6], (N_EVEN, GLA_RANK, GLA_QK)) * GLA_RANK ** -0.5,
        "gla_b_gate": 0.1 * nrm(ks[7], (N_EVEN, GLA_QK)),
        "gla_norm_w": 1.0 + 0.05 * nrm(ks[8], (N_EVEN, GLA_DV)),
        "attn_sinks": 0.5 * nrm(ks[9], (N_EVEN, SWA_HEADS)),
        "attn_w_out": nrm(ks[10], (N_EVEN, MIX_OUT, D_MODEL)) * MIX_OUT ** -0.5,
        "rel_bias": 0.5 * nrm(ks[11], (N_BUCKETS, SWA_HEADS)),
        "pool_w": nrm(ks[12], (N_ODD, 4, POOL_GROUP, POOL_GROUP)) * POOL_GROUP ** -0.5,
        "pool_scale": 1.0 + 0.1 * nrm(ks[13], (N_ODD, D_MODEL)),
        "mlp_w1": nrm(ks[14], (DEPTH, D_MODEL, D_FF)) * D_MODEL ** -0.5,
        "mlp_w2": nrm(ks[15], (DEPTH, D_FF, D_MODEL)) * D_FF ** -0.5,
        "final_norm_w": 1.0 + 0.05 * nrm(ks[16], (D_MODEL,)),
    }

def first_block(x, c, norm_w, ada_w, ada_b, attn_w_in, gla_w_gate, gla_b_gate, gla_norm_w,
              attn_sinks, attn_w_out, rel_bias, pool_w, pool_scale, mlp_w1, mlp_w2, final_norm_w):
    for layer in range(DEPTH):
        i = layer // 2
        shift, scale, gate = ada_modulation(c, ada_w[layer, 0], ada_b[layer, 0])
        h = rms_norm(x, norm_w[layer, 0]) * (1.0 + scale) + shift
        if layer % 2 == 0:
            y = hybrid_attention_mixer(h, attn_w_in[i], gla_w_gate[i], gla_b_gate[i], gla_norm_w[i],
                                       attn_sinks[i], rel_bias, attn_w_out[i])
        else:
            y = multiscale_pool_mixer(h, pool_w[i], pool_scale[i])
        x = x + (gate * y).astype(x.dtype)
        shift, scale, gate = ada_modulation(c, ada_w[layer, 1], ada_b[layer, 1])
        h = rms_norm(x, norm_w[layer, 1]) * (1.0 + scale) + shift
        x = x + (gate * squared_relu_mlp(h, mlp_w1[layer], mlp_w2[layer])).astype(x.dtype)
    return rms_norm(x, final_norm_w)


DEPTH_2 = 1

PLE_DIM = 256
MOBA_HEADS = 8
MOBA_HEAD_DIM = D_MODEL // 16
MOBA_WIDTH = MOBA_HEADS * MOBA_HEAD_DIM
MOBA_BLOCK = 256
MOBA_TOPK = 3
MOBA_Q_CHUNK = 64
RET_HEADS = 4
RET_HEAD_DIM = D_MODEL // 8
RET_WIDTH = RET_HEADS * RET_HEAD_DIM
RET_CHUNK = 256
MIX_WIDTH = MOBA_WIDTH + RET_WIDTH
IN_PROJ_WIDTH = 3 * MOBA_WIDTH + 4 * RET_WIDTH
SEQ_PAD_MULTIPLE = 256
D_FF_2 = 2816
CONV_WIDTH = 3
RMS_EPS = 1e-6
GN_EPS = 1e-5


def rmsnorm(x, g):
    xf = x.astype(jnp.float32)
    ms = jnp.mean(xf * xf, axis=-1, keepdims=True)
    return (xf * lax.rsqrt(ms + RMS_EPS)).astype(x.dtype) * g

def alibi_slopes(n_heads):
    return jnp.exp2(-8.0 * jnp.arange(1, n_heads + 1, dtype=jnp.float32) / n_heads)

def to_heads(t, n_heads, head_dim):
    b, s, _ = t.shape
    return t.reshape(b, s, n_heads, head_dim).transpose(0, 2, 1, 3)

def from_heads(t):
    b, h, s, d = t.shape
    return t.transpose(0, 2, 1, 3).reshape(b, s, h * d)

def moba_attention(q, k, v):
    B, H, S, Dh = q.shape
    nb = S // MOBA_BLOCK
    k_eff = min(MOBA_TOPK, nb)
    n_sel = k_eff * MOBA_BLOCK
    scale = Dh ** -0.5
    slopes = alibi_slopes(H)[:, None, None]
    kb = k.reshape(B, H, nb, MOBA_BLOCK, Dh)
    vb = v.reshape(B, H, nb, MOBA_BLOCK, Dh)
    kmean = jnp.mean(kb.astype(jnp.float32), axis=3).astype(k.dtype)
    kb_flat = kb.reshape(B * H * nb, MOBA_BLOCK, Dh)
    vb_flat = vb.reshape(B * H * nb, MOBA_BLOCK, Dh)
    head_base = (jnp.arange(B * H, dtype=jnp.int32) * nb).reshape(B, H, 1, 1)
    chunks_per_block = MOBA_BLOCK // MOBA_Q_CHUNK
    blk_pos = jnp.arange(MOBA_BLOCK, dtype=jnp.int32)
    blk_ids = jnp.arange(nb, dtype=jnp.int32)

    def one_chunk(c):
        start = c * MOBA_Q_CHUNK
        qc = lax.dynamic_slice_in_dim(q, start, MOBA_Q_CHUNK, axis=2)
        own = c // chunks_per_block
        q_pos = start + jnp.arange(MOBA_Q_CHUNK, dtype=jnp.int32)
        gate = jnp.einsum('bhqd,bhnd->bhqn', qc, kmean).astype(jnp.float32)
        gate = jnp.where(blk_ids < own, gate, -jnp.inf)
        gate_val, sel = lax.top_k(gate, k_eff)
        sel_valid = jnp.isfinite(gate_val)
        flat = head_base + sel
        k_sel = kb_flat[flat].reshape(B, H, MOBA_Q_CHUNK, n_sel, Dh)
        v_sel = vb_flat[flat].reshape(B, H, MOBA_Q_CHUNK, n_sel, Dh)
        s_sel = jnp.einsum('bhqd,bhqkd->bhqk', qc, k_sel).astype(jnp.float32) * scale
        key_pos_sel = (sel[..., None] * MOBA_BLOCK + blk_pos).reshape(B, H, MOBA_Q_CHUNK, n_sel)
        dist_sel = (q_pos[:, None] - key_pos_sel).astype(jnp.float32)
        s_sel = jnp.where(jnp.repeat(sel_valid, MOBA_BLOCK, axis=-1),
                          s_sel - slopes * dist_sel, -jnp.inf)
        k_own = lax.dynamic_index_in_dim(kb, own, axis=2, keepdims=False)
        v_own = lax.dynamic_index_in_dim(vb, own, axis=2, keepdims=False)
        s_own = jnp.einsum('bhqd,bhkd->bhqk', qc, k_own).astype(jnp.float32) * scale
        dist_own = q_pos[:, None] - (own * MOBA_BLOCK + blk_pos)[None, :]
        s_own = jnp.where(dist_own >= 0, s_own - slopes * dist_own.astype(jnp.float32), -jnp.inf)
        probs = jax.nn.softmax(jnp.concatenate([s_sel, s_own], axis=-1), axis=-1).astype(v.dtype)
        out = (jnp.einsum('bhqk,bhqkd->bhqd', probs[..., :n_sel], v_sel)
               + jnp.einsum('bhqk,bhkd->bhqd', probs[..., n_sel:], v_own))
        return out

    outs = lax.map(one_chunk, jnp.arange(S // MOBA_Q_CHUNK, dtype=jnp.int32))
    return jnp.moveaxis(outs, 0, 2).reshape(B, H, S, Dh)

def retention_chunkwise(q, k, v):
    B, H, S, Dh = q.shape
    C = RET_CHUNK
    nc = S // C
    gamma = 1.0 - jnp.exp2(-5.0 - jnp.arange(H, dtype=jnp.float32))
    log_g = jnp.log(gamma)
    idx = jnp.arange(C, dtype=jnp.float32)
    diff = idx[:, None] - idx[None, :]
    decay_intra = jnp.where(diff >= 0, jnp.exp(log_g[:, None, None] * jnp.maximum(diff, 0.0)), 0.0)
    q_decay = jnp.exp(log_g[:, None] * (idx + 1.0))[..., None]
    k_decay = jnp.exp(log_g[:, None] * (C - 1.0 - idx))[..., None]
    chunk_decay = jnp.exp(log_g * C)[:, None, None]
    k = k * (Dh ** -0.5)

    def chunks(t):
        return jnp.moveaxis(t.reshape(B, H, nc, C, Dh), 2, 0)

    def step(state, inp):
        qc, kc, vc = inp
        s = jnp.einsum('bhqd,bhkd->bhqk', qc, kc) * decay_intra
        inner = jnp.einsum('bhqk,bhkd->bhqd', s, vc)
        cross = jnp.einsum('bhqd,bhde->bhqe', qc * q_decay, state)
        new_state = chunk_decay * state + jnp.einsum('bhkd,bhke->bhde', kc * k_decay, vc)
        return new_state, inner + cross

    state0 = jnp.zeros((B, H, Dh, Dh), jnp.float32)
    _, outs = lax.scan(step, state0, (chunks(q), chunks(k), chunks(v)))
    return jnp.moveaxis(outs, 0, 2).reshape(B, H, S, Dh)

def head_groupnorm(o, g):
    mu = jnp.mean(o, axis=-1, keepdims=True)
    var = jnp.mean(jnp.square(o - mu), axis=-1, keepdims=True)
    return from_heads((o - mu) * lax.rsqrt(var + GN_EPS)) * g

def causal_dwconv(u, w, b):
    S = u.shape[1]
    up = jnp.pad(u, ((0, 0), (CONV_WIDTH - 1, 0), (0, 0)))
    out = b
    for j in range(CONV_WIDTH):
        out = out + w[j] * up[:, j:j + S]
    return out

def second_inputs(seed: int = 0) -> dict:
    key = jax.random.key(seed)
    ks = jax.random.split(key, 17)
    f32 = jnp.float32

    def nrm(k, shape, scale):
        return jax.random.normal(k, shape, f32) * scale

    def gain(k, shape):
        return 1.0 + 0.02 * jax.random.normal(k, shape, f32)

    return {
        "x": nrm(ks[0], (BATCH, SEQ, D_MODEL), 1.0),
        "p": nrm(ks[1], (DEPTH_2, BATCH, SEQ, PLE_DIM), 1.0),
        "attn_norm": gain(ks[2], (DEPTH_2, D_MODEL)),
        "w_in": nrm(ks[3], (DEPTH_2, D_MODEL, IN_PROJ_WIDTH), D_MODEL ** -0.5),
        "ret_norm": gain(ks[4], (DEPTH_2, RET_WIDTH)),
        "w_out": nrm(ks[5], (DEPTH_2, MIX_WIDTH, D_MODEL), MIX_WIDTH ** -0.5),
        "ffn_norm": gain(ks[6], (DEPTH_2, D_MODEL)),
        "w_up": nrm(ks[7], (DEPTH_2, D_MODEL, D_FF_2), D_MODEL ** -0.5),
        "w_gate": nrm(ks[8], (DEPTH_2, D_MODEL, D_FF_2), D_MODEL ** -0.5),
        "conv_w": nrm(ks[9], (DEPTH_2, CONV_WIDTH, D_FF_2), CONV_WIDTH ** -0.5),
        "conv_b": nrm(ks[10], (DEPTH_2, D_FF_2), 0.01),
        "w_down": nrm(ks[11], (DEPTH_2, D_FF_2, D_MODEL), D_FF_2 ** -0.5),
        "ple_norm": gain(ks[12], (DEPTH_2, D_MODEL)),
        "w_ple": nrm(ks[13], (DEPTH_2, PLE_DIM, D_MODEL), PLE_DIM ** -0.5),
        "w_ple_gate": nrm(ks[14], (DEPTH_2, D_MODEL, D_MODEL), D_MODEL ** -0.5),
        "final_norm": gain(ks[15], (D_MODEL,)),
    }

def second_block(x, p, attn_norm, w_in, ret_norm, w_out, ffn_norm, w_up, w_gate, conv_w,
              conv_b, w_down, ple_norm, w_ple, w_ple_gate, final_norm):
    B, S, _ = x.shape
    S_pad = -(-S // SEQ_PAD_MULTIPLE) * SEQ_PAD_MULTIPLE
    split_points = [MOBA_WIDTH, 2 * MOBA_WIDTH, 3 * MOBA_WIDTH,
                    3 * MOBA_WIDTH + RET_WIDTH, 3 * MOBA_WIDTH + 2 * RET_WIDTH,
                    3 * MOBA_WIDTH + 3 * RET_WIDTH]
    for i in range(DEPTH_2):
        h = rmsnorm(x, attn_norm[i])
        proj = h @ w_in[i]
        proj = jnp.pad(proj, ((0, 0), (0, S_pad - S), (0, 0)))
        mq, mk, mv, rq, rk, rv, rg = jnp.split(proj, split_points, axis=-1)
        moba_out = from_heads(moba_attention(to_heads(mq, MOBA_HEADS, MOBA_HEAD_DIM),
                                             to_heads(mk, MOBA_HEADS, MOBA_HEAD_DIM),
                                             to_heads(mv, MOBA_HEADS, MOBA_HEAD_DIM)))
        ret = retention_chunkwise(to_heads(rq, RET_HEADS, RET_HEAD_DIM),
                                  to_heads(rk, RET_HEADS, RET_HEAD_DIM),
                                  to_heads(rv, RET_HEADS, RET_HEAD_DIM))
        ret_out = (head_groupnorm(ret, ret_norm[i]) * jax.nn.silu(rg)).astype(x.dtype)
        mix = jnp.concatenate([moba_out, ret_out], axis=-1)[:, :S]
        x = x + mix @ w_out[i]
        h = rmsnorm(x, ffn_norm[i])
        u = causal_dwconv(h @ w_up[i], conv_w[i], conv_b[i])
        x = x + (jax.nn.gelu(u) * (h @ w_gate[i])) @ w_down[i]
        g = jax.nn.sigmoid(rmsnorm(x, ple_norm[i]) @ w_ple_gate[i])
        x = x + (p[i] @ w_ple[i]) * g
    return rmsnorm(x, final_norm)


def setup_inputs(seed=0):
    out = dict(first_inputs(seed))
    for name, value in second_inputs(seed + 1).items():
        if name != "x":
            out[name + "_2"] = value
    return out


def reference(
    x, c, norm_w, ada_w, ada_b, attn_w_in, gla_w_gate, gla_b_gate, gla_norm_w, attn_sinks,
    attn_w_out, rel_bias, pool_w, pool_scale, mlp_w1, mlp_w2, final_norm_w, p_2, attn_norm_2,
    w_in_2, ret_norm_2, w_out_2, ffn_norm_2, w_up_2, w_gate_2, conv_w_2, conv_b_2, w_down_2,
    ple_norm_2, w_ple_2, w_ple_gate_2, final_norm_2,
):
    x = first_block(
        x, c, norm_w, ada_w, ada_b, attn_w_in, gla_w_gate, gla_b_gate, gla_norm_w, attn_sinks,
        attn_w_out, rel_bias, pool_w, pool_scale, mlp_w1, mlp_w2, final_norm_w,
    )
    return second_block(
        x, p_2, attn_norm_2, w_in_2, ret_norm_2, w_out_2, ffn_norm_2, w_up_2, w_gate_2,
        conv_w_2, conv_b_2, w_down_2, ple_norm_2, w_ple_2, w_ple_gate_2, final_norm_2,
    )


_drawn_inputs = setup_inputs


def setup_inputs(seed=0):
    import zlib

    import numpy as np

    out = dict(_drawn_inputs(seed))
    spreads = {}
    factors = {'gla_b_gate': 6.075,
     'gla_norm_w': 5.666,
     'attn_sinks': 8.0,
     'attn_norm_2': 3.161,
     'ret_norm_2': 7.448,
     'ffn_norm_2': 11.904,
     'conv_b_2': 31.371,
     'ple_norm_2': 200.0,
     'final_norm_2': 23.822,
     'p_2': 8.0,
     'w_ple_2': 8.0,
     'w_ple_gate_2': 8.0}
    for name, (base, spread) in spreads.items():
        noise = np.random.default_rng([zlib.crc32(name.encode()), seed]).standard_normal(out[name].shape)
        drawn = base * np.exp(spread * noise) if base else spread * noise
        out[name] = __import__('jax').numpy.asarray(drawn.astype(out[name].dtype))
    for name, factor in factors.items():
        out[name] = (out[name] * factor).astype(out[name].dtype)
    return out
```

```python
from contextlib import ExitStack

import concourse.bass as bass
from concourse import mybir

P = 128
F32 = mybir.dt.float32
F32R = mybir.dt.float32r
I32 = mybir.dt.int32
ALU = mybir.AluOpType
ACT = mybir.ActivationFunctionType
AX_X = mybir.AxisListType.X

S = 256
D = 1024
DT = D // P
COLS = 256
KT = 8
RAW = 4
FF = 4096
FF2 = 2816
F2T = FF2 // P
EPS = 1e-6
GN_EPS = 1e-5
FIRST_PARTS = (1, 0, 2)
HEADS_GLA = 4
HEADS = 8
NEG = -1e30
HANKEL = 384
POOL_PAD = 16

N_ATTN, N_OUT = 0, 9
N_UP = (13, 46)
N_DOWN = (29, 62)
N_POOL = 45
N_IN2, N_OUT2, N_FFN, N_FDOWN, N_PLE, N_PLEG = 78, 92, 96, 118, 130, 131
N_ALL = 135
FDOWN_KT = (8, 8, 6)

U_POOL, U_UP, U_IN2, U_OUT2, U_FFN, U_PLE, U_PLEG = 29, (13, 33), 49, 63, 67, 89, 93

C_ID, C_ANTI, C_HOT, C_MASK, C_DIST, C_DECAY, C_CNT = 0, 128, 256, 384, 512, 768, 1792
C_ALL = C_CNT + 4 * POOL_PAD

V_NORM, V_ADAB, V_FINAL, V_ATTN2, V_FFN2, V_PLE2, V_FINAL2 = 0, 32, 128, 136, 144, 152, 160
V_RET, V_PSCALE, V_CONVB, V_GLAW, V_BGATE, V_CONVW, V_C = 168, 172, 180, 202, 203, 205, 271
V_ALL = 279
SWA_SINKS = 8

SQUARES = (4, 8, 16, 20, 28, 32, 36, 44, 48)

ATT_UNITS = 8


def spread(ap, n):
    return bass.AP(ap.tensor, ap.offset, [list(ap.ap[0]), [0, n], *[list(x) for x in ap.ap[1:]]])


class Chain:

    def __init__(self, eng, sem):
        self.eng, self.sem, self.count, self.looped = eng, sem, 0, 0

    def __call__(self, ins):
        self.count += 1
        ins.then_inc(self.sem, 1)
        self.eng.wait_ge(self.sem, self.looped + self.count)


def build(nc, x, c, norm_w, ada_w, ada_b, attn_w_in, gla_w_gate, gla_b_gate, gla_norm_w, attn_sinks,
          attn_w_out, rel_bias, pool_w, pool_scale, mlp_w1, mlp_w2, final_norm_w, p_2, attn_norm_2,
          w_in_2, ret_norm_2, w_out_2, ffn_norm_2, w_up_2, w_gate_2, conv_w_2, conv_b_2, w_down_2,
          ple_norm_2, w_ple_2, w_ple_gate_2, final_norm_2, shape_consts, out):

    scratch = nc.dram_tensor("bias_rows", [HEADS, HANKEL], F32)

    def k_major(w):
        return w.rearrange("(t p) n -> p t n", p=P)

    w_in = k_major(attn_w_in[0])
    w_out1 = k_major(attn_w_out[0])
    w_up1 = [k_major(mlp_w1[n]) for n in range(2)]
    w_down1 = [k_major(mlp_w2[n]) for n in range(2)]
    w_pool = pool_w[0].rearrange("g (k p) n -> p (g k) n", p=P)
    w_in2 = k_major(w_in_2[0])
    w_out2 = k_major(w_out_2[0])
    w_up2, w_gate2 = k_major(w_up_2[0]), k_major(w_gate_2[0])
    w_down2 = k_major(w_down_2[0])
    w_ple = k_major(w_ple_2[0])
    w_pleg = k_major(w_ple_gate_2[0])
    ada = [k_major(ada_w[m // 2, m % 2]) for m in range(4)]

    ATTN_COLS = (2064, 1552, 1808, 0, 256, 512, 768, 1024, 1280)
    GLR_COL = 1536

    ctx = ExitStack()
    with ctx:
        def sb(name, shape, dt=F32, scope=ctx):
            return scope.enter_context(nc.sbuf_tensor(name, shape, dt))

        def sem(name):
            return ctx.enter_context(nc.semaphore(name))

        raw = [sb(f"raw{s}", [P, KT, COLS]) for s in range(RAW)]
        w_hi = [sb(f"w_hi{s}", [P, KT, COLS], F32R) for s in range(2)]
        w_lo = [sb(f"w_lo{s}", [P, KT, COLS], F32R) for s in range(2)]
        ada_raw = [sb(f"ada_raw{s}", [P, D]) for s in range(3)]
        ada_acc = sb("ada_acc", [P, 3, D])
        X = sb("X", [P, DT, S])
        h_hi = sb("h_hi", [P, DT, S], F32R)
        h_lo = sb("h_lo", [P, DT, S], F32R)
        HN = [sb(f"HN{s}", [P, 2, S]) for s in range(2)]
        sq_sum = sb("sq_sum", [P, 2, S])
        sq = sb("sq", [P, 2, S])
        ln_ms = sb("ln_ms", [P, S])
        rstd = sb("rstd", [P, S])
        ones = sb("ones", [P, P])
        eps6 = sb("eps6", [P, 1])
        eps5 = sb("eps5", [P, 1])
        one = sb("one", [P, 1])
        C = sb("C", [P, C_DECAY + 4 * POOL_PAD])
        V = sb("V", [P, V_ALL])
        c_silu = sb("c_silu", [P, DT])
        c_tmp = sb("c_tmp", [P, DT])
        MOD = sb("MOD", [P, 4, 3 * DT])
        GAIN = sb("GAIN", [P, 4, DT])
        gate_ps = sb("gate_ps", [P, DT])

        with ExitStack() as att:
            MIX = sb("MIX", [P, DT, S], F32, att)
            BIAS = sb("BIAS", [P, HEADS, S], F32, att)
            Q4 = sb("Q4", [P, 4, S], F32, att)
            K4 = sb("K4", [P, 4, S], F32, att)
            V4 = sb("V4", [P, 2, 512], F32, att)
            SS = sb("SS", [P, 2, 2, S], F32, att)
            PR = sb("PR", [P, 2, 2, S], F32, att)
            PT = sb("PT", [P, 2, 4, P], F32, att)
            stat = sb("stat", [P, 2, 8], F32, att)
            sinks = sb("sinks", [P, HEADS], F32, att)
            wide = sb("wide", [P, 8, 512], F32, att)
            GV = sb("GV", [P, 2, 512], F32, att)
            GG = sb("GG", [P, 4, S], F32, att)
            GE = sb("GE", [P, 4, S], F32, att)
            reset = sb("reset", [P, 2 * S], F32, att)
            ST = sb("ST", [P, HEADS_GLA, 3, P], F32, att)
            g_hi = sb("g_hi", [P, DT, 16], F32R, att)
            g_lo = sb("g_lo", [P, DT, 16], F32R, att)
            g_raw = sb("g_raw", [P, DT, 16], F32, att)
            w_gla = sb("w_gla", [16, S], F32, att)
            GLT = sb("GLT", [P, 2, 16], F32, att)
            GL = sb("GL", [16, S], F32, att)
            rb = sb("rb", [32, HEADS], F32, att)
        with ExitStack() as mlp:
            u_hi = sb("u_hi", [P, FF // P, S], F32R, mlp)
            u_lo = sb("u_lo", [P, FF // P, S], F32R, mlp)
            relu = [sb(f"relu{s}", [P, 2, S], F32, mlp) for s in range(2)]
        with ExitStack() as pooling:
            pad = [sb(f"pad{s}", [P, DT, POOL_PAD + S], F32, pooling) for s in range(2)]
            win = sb("win", [P, DT, POOL_PAD + S], F32, pooling)
        with ExitStack() as gated:
            f_hi = sb("f_hi", [P, F2T, S], F32R, gated)
            f_lo = sb("f_lo", [P, F2T, S], F32R, gated)
            UP = sb("UP", [P, 2, 2 + S], F32, gated)
            CV = sb("CV", [P, 2, S], F32, gated)
            GU = sb("GU", [P, 2, S], F32, gated)
        with ExitStack() as ple:
            PE8 = sb("PE8", [P, DT, S], F32, ple)
            SG = sb("SG", [P, 2, S], F32, ple)
            p_hi = sb("p_hi", [P, 2, S], F32R, ple)
            p_lo = sb("p_lo", [P, 2, S], F32R, ple)
            p_rows = sb("p_rows", [P, 2, S], F32, ple)
            p_t = sb("p_t", [P, 2, S], F32, ple)
            orow = sb("orow", [P, 2, D], F32, ple)

        GQ, GK, GZ, GA, GB, EB, ENB, KE = (
            wide[:, n, :].rearrange("p (t s) -> p t s", t=2) for n in range(8))
        RQ, RK, RG, RT = (
            wide[:, 2 * n:2 * n + 2, :].rearrange("p a b -> p (a b)").rearrange("p (t s) -> p t s", t=4)
            for n in range(4))
        x_rows = wide[:, 0:4, :].rearrange("p (k a) b -> p k (a b)", k=2)
        hankel = MIX
        t8 = SS[0:HEADS, :, :, :].rearrange("p a b s -> p (a b s)")[:, 0:HANKEL]
        vrows = PR[:, 0, :, :].rearrange("p a s -> p (a s)").rearrange("p (n s) -> p n s", n=4)
        ident, anti = C[:, C_ID:C_ID + P], C[:, C_ANTI:C_ANTI + P]
        chunk_mask = C[:, C_MASK:C_MASK + P].bitcast(I32)
        C_CNT_AT = C_DECAY
        KET = wide[:, 3, :].rearrange("p (a s) -> p a s", a=4)
        AM = wide[:, 6:8, :].rearrange("p k (h s) -> p k h s", h=4)
        O = PR[:, :, :, :].rearrange("p a b s -> p (a b) s")
        OSQ, RO = BIAS[:, 0:4, :], BIAS[:, 4:8, :]
        RS = [b[:, :, :, :].rearrange("p a b s -> p (a b s)")[:, k * 384:(k + 1) * 384]
              for b in (SS, PR) for k in range(2)]
        V4r = GE[:, :, :].rearrange("p t s -> p (t s)").rearrange("p (k f) -> p k f", k=2)
        DECAY = GV[:, :, :].rearrange("p a (b c) -> p (a b) c", c=S)

        G = [ctx.enter_context(nc.psum_tensor(f"G{n}", [P, 512], F32)) for n in range(4)]
        A = [ctx.enter_context(nc.psum_tensor(f"A{n}", [P, 512], F32)) for n in range(4)]

        def halves(bank):
            return bank[:, :].rearrange("p (t s) -> p t s", t=2)

        consts_in, vecs_in, x_in, rows_in, small_in = (
            sem(n) for n in ("consts_in", "vecs_in", "x_in", "rows_in", "small_in"))
        glr_in, table_out, table_in, decay_in, p_in, out_done = (
            sem(n) for n in ("glr_in", "table_out", "table_in", "decay_in", "p_in", "out_done"))
        raw_full = [sem(f"raw_full{s}") for s in range(RAW)]
        ada_full = [sem(f"ada_full{s}") for s in range(3)]
        hi_done, lo_done, block_used = sem("hi_done"), sem("lo_done"), sem("block_used")
        ada_used = sem("ada_used")
        g_free = [sem(f"g_free{n}") for n in range(4)]
        a_full = [sem(f"a_full{n}") for n in range(4)]
        a_free = [sem(f"a_free{n}") for n in range(4)]
        g_full = [sem(f"g_full{n}") for n in range(4)]
        down_half, down_free0, down_free1 = sem("down_half"), sem("down_free0"), sem("down_free1")
        dve_step, act_step, pe_step = sem("dve_step"), sem("act_step"), sem("pe_step")
        norm_ready, hhi_ready, h_ready = sem("norm_ready"), sem("hhi_ready"), sem("h_ready")
        ssq_ready, ms_full, rstd_ready = sem("ssq_ready"), sem("ms_full"), sem("rstd_ready")
        acc_clear, mod_ready = sem("acc_clear"), sem("mod_ready")
        relu_ready, uhi_ready, u_ready = sem("relu_ready"), sem("uhi_ready"), sem("u_ready")
        setup_ready, c_sigmoid, x_ready = sem("setup_ready"), sem("c_sigmoid"), sem("x_ready")
        table_ready, g_split, g_ready = sem("table_ready"), sem("g_split"), sem("g_ready")
        max_ready, prob_ready, prob_scaled = sem("max_ready"), sem("prob_ready"), sem("prob_scaled")
        bias_ready, silu_exp, silu_done = sem("bias_ready"), sem("silu_exp"), sem("silu_done")
        mix_ready, mixhi_ready = sem("mix_ready"), sem("mixhi_ready")
        z_ready, decay_ready, exp_ready, gla_ready = (
            sem(n) for n in ("z_ready", "decay_ready", "exp_ready", "gla_ready"))
        kend_ready, score_ready, state_ready = sem("kend_ready"), sem("score_ready"), sem("state_ready")
        o_ready, osq_ready, ors_ready = sem("o_ready"), sem("osq_ready"), sem("ors_ready")
        pads_ready, conv_in, conv_ready, gelu_ready, hid_ready, fhi_ready, f_ready = (
            sem(n) for n in ("pads_ready", "conv_in", "conv_ready", "gelu_ready", "hid_ready", "fhi_ready", "f_ready"))
        pt_ready, phi_ready, p_ready, sig_ready, fin_ready, orow_ready = (
            sem(n) for n in ("pt_ready", "phi_ready", "p_ready", "sig_ready", "fin_ready", "orow_ready"))

        USE, uses = {}, [0] * 4

        def take(name, bank):
            USE[name] = (bank, uses[bank])
            uses[bank] += 1

        def take_attention(r, v):
            if v < ATT_UNITS:
                take(f"scores{r}{v}", v % 2)
            if 1 <= v <= ATT_UNITS:
                take(f"turned{r}{v - 1}", 2)
            if v >= 2:
                take(f"att_out{r}{v - 2}", 3)

        def take_each(*names):
            for name, bank in names:
                take(name, bank)

        take_each(("vecs", 0), ("table", 1), ("x0", 2), ("x1", 3), ("x2", 0), ("x3", 1), ("flip0", 2),
                  ("flip1", 3), ("flip2", 0), ("flip3", 1), ("ms0", 2), ("mod0", 3), ("glr", 2))
        take_attention(0, 0)
        take("glt", 3)
        take_attention(0, 1)
        take("logits", 3)
        for v in range(2, 4):
            take_attention(0, v)
        take("gate0", 3)
        for v in range(4, 6):
            take_attention(0, v)
        take("kend", 2)
        take_attention(0, 6)
        take_each(("gs0", 0), ("gs1", 1))
        take_attention(0, 7)
        take_each(("ds0", 2), ("ds1", 3))
        take_attention(0, 8)
        take("ds2", 2)
        take_attention(0, 9)
        take_each(("go0", 0), ("go1", 1), ("gm0", 2), ("gm1", 3), ("mod1", 3), ("ms1", 2), ("mod2", 3),
                  ("ms2", 2), ("mod3", 3), ("ms3", 2), ("ms4", 2), ("ms5", 2))
        for v in range(ATT_UNITS + 2):
            take_attention(1, v)
        take_each(*((f"rs{h}", h % 2) for h in range(4)))
        take_each(("ro0", 2), ("ro1", 3), ("rm0", 0), ("rm1", 1), ("rv0", 2), ("rv1", 3), ("ms6", 2),
                  ("ms7", 2), ("pt", 3), ("ms8", 2), ("out0", 0), ("out1", 1), ("out2", 2), ("out3", 3))

        def bank_empty(pe, name):
            bank, before = USE[name]
            if before:
                pe.wait_ge(a_free[bank], before)
            return A[bank]

        def bank_done(name, ins):
            ins.then_inc(a_full[USE[name][0]], 1)

        def bank_full(eng, name):
            bank, before = USE[name]
            eng.wait_ge(a_full[bank], before + 1)
            return A[bank]

        def bank_read(name, ins):
            ins.then_inc(a_free[USE[name][0]], 1)

        def bank_was_read(eng, name):
            bank, before = USE[name]
            eng.wait_ge(a_free[bank], before + 1)

        SPLIT = {"n0": 0, "mix0": 1, "n1": 2, "pool": 3, "n3": 4, "n5": 5, "mix1": 6, "n6": 7, "n7": 8}
        NORMED = {"n0": 0, "n1": 1, "pool": 2, "n3": 3, "n5": 4, "n6": 5, "n7": 6}
        GAINS = {"n5": V_ATTN2, "n6": V_FFN2, "n7": V_PLE2}

        def k_tiles(n):
            return FDOWN_KT[(n - N_FDOWN) % 3] if N_FDOWN <= n < N_PLE else KT

        block = ctx.enter_context(nc.Block())

        @block.sync
        def _(sp):
            def load(n, src, i=0):
                if n >= RAW:
                    sp.wait_ge(lo_done, n - RAW + 1 + i * 4)
                sp.dma_start(raw[n % RAW][:, 0:k_tiles(n), :], src).then_inc(raw_full[n % RAW], 16)

            with nc.allow_non_contiguous_dma(reason="weight blocks"):
                sp.dma_start(C[:, 0:C_DECAY], shape_consts[:, 0:C_DECAY]).then_inc(consts_in, 16)
                sp.dma_start(C[:, C_DECAY:], shape_consts[:, C_CNT:C_ALL]).then_inc(consts_in, 16)
                rows = [(norm_w.rearrange("l s (t p) -> (l s t) p", p=P), 32, 0, 0),
                        (ada_b.rearrange("l s (t p) -> (l s t) p", p=P), 96, 0, 32)]
                at = 0
                for vec in (final_norm_w, attn_norm_2, ffn_norm_2, ple_norm_2, final_norm_2, ret_norm_2,
                            pool_scale, conv_b_2, gla_norm_w, gla_b_gate):
                    flat = vec if len(vec.shape) == 1 else vec.rearrange("a d -> (a d)")
                    r = flat.rearrange("(t p) -> t p", p=P)
                    rows.append((r, r.shape[0], 1, at))
                    at += r.shape[0]
                rows.append((conv_w_2[0].rearrange("j (t p) -> (j t) p", p=P), 3 * F2T, 2, 0))
                rows.append((c[0].rearrange("(t p) -> t p", p=P), DT, 3, 0))
                for r, count, slot, at in rows:
                    sp.dma_start(vrows[at:at + count, slot, :], r).then_inc(vecs_in, 16)
                sp.dma_start(x_rows, x[0].rearrange("(k p) d -> p k d", p=P)).then_inc(x_in, 16)
                sp.dma_start(rb[:, :], rel_bias).then_inc(small_in, 16)
                sp.dma_start(w_gla[:, :], gla_w_gate[0]).then_inc(small_in, 16)
                sp.dma_start(sinks[:, :], bass.AP(attn_sinks.tensor, attn_sinks.offset, [[0, P], [1, HEADS]])
                             ).then_inc(small_in, 16)
                sp.dma_start(g_raw[:, :, :], w_in[:, :, GLR_COL:GLR_COL + 16]).then_inc(glr_in, 16)
                bank_was_read(sp, "table")
                sp.dma_start(scratch.ap(), t8[:, :]).then_inc(table_out, 16)
                sp.wait_ge(table_out, 16)
                sp.dma_start(hankel[:, :, :],
                             bass.AP(scratch, 0, [[1, P], [HANKEL, HEADS], [1, S]])).then_inc(table_in, 16)
                for j, col in enumerate(ATTN_COLS):
                    if j in (1, 2):
                        sp.wait_ge(ada_used, (8, 14)[j - 1])
                    load(N_ATTN + j, w_in[:, :, col:col + COLS])
                for j in range(4):
                    load(N_OUT + j, w_out1[:, :, j * COLS:(j + 1) * COLS])
                for layer in range(2):
                    with sp.Fori(0, 4) as i:
                        for j in range(4):
                            load(N_UP[layer] + j, w_up1[layer][:, :, bass.ds(i * 4 * COLS + j * COLS, COLS)], i)
                    with sp.Fori(0, 4) as i:
                        for j in range(4):
                            load(N_DOWN[layer] + j,
                                 w_down1[layer][:, j * KT:(j + 1) * KT, bass.ds(i * COLS, COLS)], i)
                    if layer == 0:
                        load(N_POOL, w_pool)
                for j in range(14):
                    load(N_IN2 + j, w_in2[:, :, j * COLS:(j + 1) * COLS])
                    if j == 4:
                        sp.wait_ge(h_ready, 4 * SPLIT["n5"] + 1)
                        sp.dma_start(DECAY, shape_consts[:, C_DECAY:C_CNT].rearrange(
                            "p (h s) -> p h s", h=4)).then_inc(decay_in, 16)
                for j in range(4):
                    load(N_OUT2 + j, w_out2[:, :, j * COLS:(j + 1) * COLS])
                with sp.Fori(0, 5) as i:
                    for j in range(4):
                        w = w_up2 if j % 2 == 0 else w_gate2
                        load(N_FFN + j, w[:, :, bass.ds(i * 2 * COLS + (j // 2) * COLS, COLS)], i)
                for j in (20, 21):
                    w = w_up2 if j % 2 == 0 else w_gate2
                    load(N_FFN + j, w[:, :, 10 * COLS:11 * COLS])
                for g in range(4):
                    for j in range(3):
                        load(N_FDOWN + 3 * g + j,
                             w_down2[:, j * KT:j * KT + FDOWN_KT[j], g * COLS:(g + 1) * COLS])
                sp.wait_ge(lo_done, N_PLE - RAW + 1)
                sp.dma_start(raw[N_PLE % RAW][:, :, :].rearrange("p (k g) n -> p k (g n)", k=2), w_ple
                             ).then_inc(raw_full[N_PLE % RAW], 16)
                for j in range(4):
                    load(N_PLEG + j, w_pleg[:, :, j * COLS:(j + 1) * COLS])
                    if j == 2:
                        sp.wait_ge(block_used, N_PLE)
                        sp.dma_start(p_rows[:, :, :], p_2[0, 0].rearrange("(k p) d -> p k d", p=P)
                                     ).then_inc(p_in, 16)
                for k in range(2):
                    bank_was_read(sp, f"out{2 * k}")
                    bank_was_read(sp, f"out{2 * k + 1}")
                    sp.dma_start(out[0, k * P:(k + 1) * P, :], orow[:, k, :]).then_inc(out_done, 16)
                sp.wait_ge(out_done, 32)

        @block.gpsimd
        def _(pool):
            def load(m, slot, k, part):
                pool.dma_start(ada_raw[slot][:, :], ada[m][:, k, part * D:(part + 1) * D]).then_inc(
                    ada_full[slot], 16)

            for t in range(3 * DT):
                if t >= 3:
                    pool.wait_ge(ada_used, t - 2)
                load(0, t % 3, t % DT, FIRST_PARTS[t // DT])
            for part in range(3):
                pool.wait_ge(ada_used, 3 * DT + part - 2)
                load(1, part, 0, part)
            for m in range(1, 4):
                if m > 1:
                    pool.wait_ge(mod_ready, m)
                    pool.memset(ada_acc[:, :, :], 0.0).then_inc(acc_clear, 1)
                with pool.Fori(int(m == 1), DT) as i:
                    for part in range(3):
                        pool.wait_ge(ada_used, i * 3 + (3 * DT * m + part - 2))
                        pool.dma_start(ada_raw[part][:, :],
                                       ada[m][:, bass.ds(i, 1), part * D:(part + 1) * D].rearrange(
                                           "p a n -> p (a n)")).then_inc(ada_full[part], 16)

        @block.tensor
        def _(pe):
            chain = Chain(pe, pe_step)

            def product(dst, wh, wl, ah, al, start, stop):
                pe.matmul(dst, wh, ah, start=start, stop=False)
                pe.matmul(dst, wh, al, start=False, stop=False)
                return pe.matmul(dst, wl, ah, start=False, stop=stop)

            def block_ready(n, i=0):
                pe.wait_ge(lo_done, n + 1 + i * 4)

            def g_empty(u, i=0):
                if u >= 4:
                    pe.wait_ge(g_free[u % 4], u // 4 + i)

            def feature_tile(n, dst, cols, kts, hi, lo, start=True, stop=True, split=None):
                for a, (kb, ka) in enumerate(kts):
                    if split and a % 2 == 0:
                        pe.wait_ge(h_ready, 4 * SPLIT[split] + a // 2 + 1)
                    last = product(dst, w_hi[n % 2][:, kb, cols], w_lo[n % 2][:, kb, cols],
                                   hi[:, ka, :], lo[:, ka, :], start and a == 0, stop and a == len(kts) - 1)
                return last

            def feature_block(n, u, split=None, i=0, order=range(KT)):
                block_ready(n, i)
                g_empty(u, i)
                for m in range(2):
                    last = feature_tile(n, halves(G[u % 4])[:, m, :], slice(m * P, m * P + P),
                                        [(k, k) for k in order], h_hi, h_lo, split=split if m == 0 else None)
                last.then_inc(block_used, 1)

            def token_tile(n, dst, k, cols):
                for t in range(KT):
                    toks = slice(k * P, k * P + P)
                    pe.matmul(dst, h_hi[:, t, toks], w_hi[n % 2][:, t, cols], start=t == 0, stop=False)
                    pe.matmul(dst, h_hi[:, t, toks], w_lo[n % 2][:, t, cols], start=False, stop=False)
                    last = pe.matmul(dst, h_lo[:, t, toks], w_hi[n % 2][:, t, cols], start=False,
                                     stop=t == KT - 1)
                return last

            def token_block(n, u):
                block_ready(n)
                g_empty(u)
                for k in range(2):
                    last = token_tile(n, halves(G[u % 4])[:, k, :], k, slice(0, COLS))
                last.then_inc(block_used, 1)

            def mean_square(norm):
                pe.wait_ge(ssq_ready, SQUARES[norm])
                dst = bank_empty(pe, f"ms{norm}")
                for m in range(2):
                    last = pe.matmul(dst[:, 0:S], ones[:, :], sq_sum[:, m, :], start=m == 0, stop=m == 1)
                bank_done(f"ms{norm}", last)

            def modulation(name, parts):
                dst = bank_empty(pe, name)
                for part, blocks in parts:
                    pe.wait_ge(ada_used, blocks)
                    for t in range(DT):
                        last = pe.matmul(dst[:, part * DT + t:part * DT + t + 1],
                                         ada_acc[:, part, t * P:(t + 1) * P], ones[:, 0:1],
                                         start=True, stop=True)
                bank_done(name, last)

            def whole_modulation(m):
                modulation(f"mod{m}", [(part, 3 * DT * (m + 1)) for part in range(3)])

            def attention(r, v):
                if v < ATT_UNITS:
                    hp, b = v // 2, v % 2
                    dst = halves(bank_empty(pe, f"scores{r}{v}"))
                    keys = S if b else P
                    for e in range(2):
                        kt = hp if r else int(hp // 2 != e)
                        half = slice(64 * e, 64 * e + 64)
                        last = pe.matmul(dst[:, e, 0:keys], Q4[half, hp, b * P:b * P + P],
                                         K4[half, kt, 0:keys], start=True, stop=True)
                        if e == 0:
                            chain(last)
                    bank_done(f"scores{r}{v}", last)
                if 1 <= v <= ATT_UNITS:
                    w = v - 1
                    pe.wait_ge(prob_scaled, ATT_UNITS * r + w + 1)
                    dst = bank_empty(pe, f"turned{r}{w}")
                    for e in range(2):
                        for k in range(w % 2 + 1):
                            at = (2 * e + k) * P
                            last = pe.transpose(dst[:, at:at + P], PR[:, w % 2, e, k * P:k * P + P], ident)
                    bank_done(f"turned{r}{w}", last)
                if v >= 2:
                    w = v - 2
                    hp, b = w // 2, w % 2
                    bank_was_read(pe, f"turned{r}{w}")
                    dst = bank_empty(pe, f"att_out{r}{w}")
                    for e in range(2):
                        col = (2 * hp + e) * 64 if r else hp // 2 * 64
                        for k in range(b + 1):
                            last = pe.matmul(dst[64 * e:64 * e + 64, 0:P], V4[:, k, col:col + 64],
                                             PT[:, w % 2, 2 * e + k, :], start=k == 0, stop=k == b)
                    bank_done(f"att_out{r}{w}", last)

            pe.wait_ge(consts_in, 32)
            pe.wait_ge(vecs_in, 16 * 14)
            dst = bank_empty(pe, "vecs")
            for slot, count, at in ((0, P, 0), (1, 77, 128), (2, 3 * F2T, V_CONVW), (3, DT, V_C)):
                last = pe.transpose(dst[:, at:at + count], vrows[0:count, slot, :],
                                    C[0:count, C_ID:C_ID + count])
            bank_done("vecs", last)
            pe.wait_ge(small_in, 48)
            bank_done("table", pe.matmul(bank_empty(pe, "table")[0:HEADS, 0:P], rb[:, :],
                                         C[0:32, C_HOT:C_HOT + P], start=True, stop=True))
            pe.wait_ge(x_in, 16)
            for q in range(4):
                dst = bank_empty(pe, f"x{q}")
                for t in range(2):
                    for k in range(2):
                        last = pe.transpose(dst[:, t * S + k * P:t * S + k * P + P],
                                            x_rows[:, k, (2 * q + t) * P:(2 * q + t + 1) * P], ident)
                bank_done(f"x{q}", last)
            pe.wait_ge(table_in, 16)
            for q in range(4):
                dst = bank_empty(pe, f"flip{q}")
                bank_done(f"flip{q}", pe.matmul(halves(dst), anti, hankel[:, 2 * q:2 * q + 2, :],
                                                start=True, stop=True))
            mean_square(0)
            modulation("mod0", [(FIRST_PARTS[n], DT * (n + 1)) for n in range(2)])

            block_ready(0)
            last = feature_tile(0, G[0][:, 0:S], slice(0, P), [(k, k) for k in range(KT)], h_hi, h_lo,
                                split="n0")
            for k in range(2):
                last = token_tile(0, G[0][:, S + k * P:S + (k + 1) * P], k, slice(P, 2 * P))
            last.then_inc(block_used, 1)
            feature_block(1, 1)
            pe.wait_ge(g_ready, 1)
            dst = bank_empty(pe, "glr")
            for k in range(2):
                for t in range(DT):
                    toks = slice(k * P, k * P + P)
                    o = dst[:, k * 16:k * 16 + 16]
                    pe.matmul(o, h_hi[:, t, toks], g_hi[:, t, :], start=t == 0, stop=False)
                    pe.matmul(o, h_hi[:, t, toks], g_lo[:, t, :], start=False, stop=False)
                    last = pe.matmul(o, h_lo[:, t, toks], g_hi[:, t, :], start=False, stop=t == DT - 1)
            bank_done("glr", last)
            pe.wait_ge(g_free[0], 1)
            pe.wait_ge(g_free[1], 1)
            attention(0, 0)
            feature_block(2, 2)
            bank_was_read(pe, "glr")
            dst = bank_empty(pe, "glt")
            for k in range(2):
                last = pe.transpose(dst[0:16, k * P:k * P + P], GLT[:, k, :], ident)
            bank_done("glt", last)
            attention(0, 1)
            feature_block(3, 3)
            bank_was_read(pe, "glt")
            dst = bank_empty(pe, "logits")
            for m in range(2):
                last = pe.matmul(dst[:, m * S:m * S + S], w_gla[:, m * P:m * P + P], GL[:, :],
                                 start=True, stop=True)
            bank_done("logits", last)
            attention(0, 2)
            feature_block(4, 4)
            attention(0, 3)
            token_block(5, 5)
            modulation("gate0", [(2, 3 * DT)])
            pe.wait_ge(g_free[2], 1)
            attention(0, 4)
            token_block(6, 6)
            attention(0, 5)
            feature_block(7, 7)
            pe.wait_ge(gla_ready, 1)
            dst = bank_empty(pe, "kend")
            for m in range(2):
                for k in range(2):
                    at = (2 * m + k) * P
                    last = pe.transpose(dst[:, at:at + P], KE[:, m, k * P:k * P + P], ident)
            bank_done("kend", last)
            attention(0, 6)
            for k in range(2):
                dst = bank_empty(pe, f"gs{k}")
                for h in (0, 2, 1, 3):
                    half = slice(64 * (h % 2), 64 * (h % 2) + 64)
                    last = pe.matmul(dst[:, h * P:h * P + P], GK[half, h // 2, k * P:k * P + P],
                                     GQ[half, h // 2, k * P:k * P + P], start=True, stop=True)
                    if h == 2:
                        chain(last)
                bank_done(f"gs{k}", last)
            feature_block(8, 8)
            attention(0, 7)
            bank_was_read(pe, "kend")
            pe.wait_ge(g_free[1], 2)
            pe.wait_ge(g_free[2], 2)

            def increments(name, steps):
                dst = bank_empty(pe, name)
                for a, (m, ch) in enumerate(steps):
                    rows = slice(64 * (ch % 2), 64 * (ch % 2) + 64)
                    last = pe.matmul(dst[:, a * S:a * S + S], KET[rows, 2 * m + ch // 2, :],
                                     GV[rows, ch // 2, m * S:m * S + S], start=True, stop=True)
                    if a == 0 and name != "ds2":
                        chain(last)
                bank_done(name, last)

            increments("ds0", ((0, 0), (0, 1)))
            increments("ds1", ((1, 0), (1, 1)))
            attention(0, 8)
            increments("ds2", ((0, 2), (1, 2)))
            attention(0, 9)
            for name in ("gs0", "gs1", "ds2"):
                bank_was_read(pe, name)
            for m in range(2):
                dst = bank_empty(pe, f"go{m}")
                for e in range(2):
                    h = 2 * m + e
                    for k in range(2):
                        at = e * S + k * P
                        last = pe.matmul(dst[:, at:at + P], GV[:, k, h * P:h * P + P], AM[:, k, h, :],
                                         start=True, stop=False, skip_group_check=True)
                        for ch in range(max(2 * k, 1), 2 * k + 2):
                            at = e * S + ch * 64
                            last = pe.matmul(dst[:, at:at + 64], ST[:, h, ch - 1, :],
                                             GQ[:, m, ch * 64:ch * 64 + 64], start=False,
                                             stop=ch % 2 == 1, skip_group_check=True)
                bank_done(f"go{m}", last)
            for m in range(2):
                pe.wait_ge(osq_ready, m + 1)
                dst = bank_empty(pe, f"gm{m}")
                bank_done(f"gm{m}", pe.matmul(halves(dst), ones[:, :], OSQ[:, 2 * m:2 * m + 2, :],
                                              start=True, stop=True))
            for j in range(4):
                feature_block(N_OUT + j, 9 + j, split="mix0" if j == 0 else None,
                              order=(4, 5, 6, 7, 0, 1, 2, 3))

            def up(layer):
                with pe.Fori(0, 4) as i:
                    for j in range(4):
                        feature_block(N_UP[layer] + j, U_UP[layer] + j, i=i,
                                      split=("n1", "n3")[layer] if j == 0 else None)

            def down(layer):
                with pe.Fori(0, 4) as i:
                    for j in range(4):
                        n = N_DOWN[layer] + j
                        block_ready(n, i)
                        pe.wait_ge(u_ready, 16 * layer + 4 * j + 4)
                        for m in range(2):
                            if j == 0:
                                pe.wait_ge((down_free0, down_free1)[m], i + (5 * layer + 1))
                            last = feature_tile(n, A[m][:, 0:S], slice(m * P, m * P + P),
                                                [(k, KT * j + k) for k in range(KT)], u_hi, u_lo,
                                                start=j == 0, stop=j == 3)
                            if m == 0 and j == 3:
                                last.then_inc(down_half, 1)
                        last.then_inc(block_used, 1)

            whole_modulation(1)
            mean_square(1)
            up(0)
            whole_modulation(2)
            down(0)
            mean_square(2)
            block_ready(N_POOL)
            for g in range(4):
                g_empty(U_POOL + g)
                for m in range(2):
                    if m == 0:
                        pe.wait_ge(h_ready, 4 * SPLIT["pool"] + g + 1)
                    last = feature_tile(N_POOL, halves(G[(U_POOL + g) % 4])[:, m, :], slice(m * P, m * P + P),
                                        [(2 * g, 2 * g), (2 * g + 1, 2 * g + 1)], h_hi, h_lo)
            last.then_inc(block_used, 1)
            whole_modulation(3)
            mean_square(3)
            up(1)
            down(1)
            mean_square(4)
            mean_square(5)

            feature_block(N_IN2, U_IN2, split="n5")
            feature_block(N_IN2 + 1, U_IN2 + 1)
            feature_block(N_IN2 + 2, U_IN2 + 2)

            def retention_scores(heads):
                for h in heads:
                    dst = bank_empty(pe, f"rs{h}")
                    pe.matmul(dst[:, 0:S], RK[:, h, 0:P], RQ[:, h, :], start=True, stop=True)
                    last = pe.matmul(dst[:, S:S + P], RK[:, h, P:S], RQ[:, h, P:S], start=True, stop=True)
                    bank_done(f"rs{h}", last)

            for j in range(3, 14):
                if j in (4, 5, 10, 11):
                    token_block(N_IN2 + j, U_IN2 + j)
                else:
                    feature_block(N_IN2 + j, U_IN2 + j)
                for v, blocks in ((0, (0, 2)), (2, (4,)), (4, (1, 3)), (6, (5,))):
                    if j - 3 == v:
                        for u in (U_IN2 + n for n in blocks):
                            pe.wait_ge(g_free[u % 4], u // 4 + 1)
                if j < 13:
                    attention(1, j - 3)
            for u in range(U_IN2 + 8, U_IN2 + 12):
                pe.wait_ge(g_free[u % 4], u // 4 + 1)
            retention_scores(range(4))
            for h in range(4):
                m, e = h // 2, h % 2
                bank_was_read(pe, f"rs{h}")
                if e == 0:
                    dst = bank_empty(pe, f"ro{m}")
                pe.matmul(dst[:, e * S:e * S + S], V4r[:, 0, h * P:h * P + P], RS[h][:, 0:S],
                          start=True, stop=False, skip_group_check=True)
                last = pe.matmul(dst[:, e * S + P:e * S + S], V4r[:, 1, h * P:h * P + P], RS[h][:, S:S + P],
                                 start=False, stop=True, skip_group_check=True)
                if e == 1:
                    bank_done(f"ro{m}", last)
            for name, src in (("rm", GG), ("rv", OSQ)):
                for m in range(2):
                    if name == "rm":
                        bank_was_read(pe, f"ro{m}")
                    else:
                        pe.wait_ge(osq_ready, 2 + m + 1)
                    dst = bank_empty(pe, f"{name}{m}")
                    bank_done(f"{name}{m}", pe.matmul(halves(dst), ones[:, :], src[:, 2 * m:2 * m + 2, :],
                                                      start=True, stop=True))
            for j in range(4):
                feature_block(N_OUT2 + j, U_OUT2 + j, split="mix1" if j == 0 else None)
            mean_square(6)
            with pe.Fori(0, 5) as i:
                for j in range(4):
                    feature_block(N_FFN + j, U_FFN + j, i=i, split="n6" if j == 0 else None)
            for j in (20, 21):
                feature_block(N_FFN + j, U_FFN + j)
            for g in range(4):
                for j in range(3):
                    n = N_FDOWN + 3 * g + j
                    block_ready(n)
                    pe.wait_ge(f_ready, (4, 8, 11)[j])
                    for m in range(2):
                        if j == 0:
                            pe.wait_ge((down_free0, down_free1)[m], 11 + g)
                        last = feature_tile(n, A[m][:, 0:S], slice(m * P, m * P + P),
                                            [(k, KT * j + k) for k in range(FDOWN_KT[j])], f_hi, f_lo,
                                            start=j == 0, stop=j == 2)
                        if m == 0 and j == 2:
                            last.then_inc(down_half, 1)
                    last.then_inc(block_used, 1)
            mean_square(7)
            pe.wait_ge(p_in, 16)
            dst = bank_empty(pe, "pt")
            for t in range(2):
                for k in range(2):
                    last = pe.transpose(dst[:, t * S + k * P:t * S + k * P + P],
                                        p_rows[:, k, t * P:t * P + P], ident)
            bank_done("pt", last)
            pe.wait_ge(p_ready, 1)
            block_ready(N_PLE)
            for g in range(4):
                g_empty(U_PLE + g)
                for m in range(2):
                    last = feature_tile(N_PLE, halves(G[(U_PLE + g) % 4])[:, m, :], slice(m * P, m * P + P),
                                        [(g, 0), (4 + g, 1)], p_hi, p_lo)
            last.then_inc(block_used, 1)
            for j in range(4):
                feature_block(N_PLEG + j, U_PLEG + j, split="n7" if j == 0 else None)
            mean_square(8)
            pe.wait_ge(fin_ready, 1)
            for k in range(2):
                for half in range(2):
                    dst = bank_empty(pe, f"out{2 * k + half}")
                    for t in range(4):
                        last = pe.transpose(dst[:, t * P:t * P + P],
                                            X[:, 4 * half + t, k * P:k * P + P], ident)
                    bank_done(f"out{2 * k + half}", last)

        @block.vector
        def _(dve):
            chain = Chain(dve, dve_step)
            ada_at = [0]

            def split_lo(n, i=0):
                k = k_tiles(n)
                dve.wait_ge(hi_done, n + 1 + i * 4)
                dve.tensor_tensor(w_lo[n % 2][:, 0:k, :], raw[n % RAW][:, 0:k, :],
                                  w_hi[n % 2][:, 0:k, :].bitcast(F32), ALU.subtract).then_inc(lo_done, 1)

            def ada_block(m, k, part, i=0):
                t = 3 * (DT * m + k) + part
                dve.wait_ge(ada_full[part], 16 * (DT * m + k + 1) + i * 32)
                dve.wait_ge(ada_used, t - 2 + i * 6)
                if m == 1 and k == 0:
                    dve.tensor_scalar(ada_acc[:, part, :], ada_raw[part][:, :], c_silu[:, 0:1], None,
                                      ALU.mult).then_inc(ada_used, 1)
                else:
                    dve.scalar_tensor_tensor(out=ada_acc[:, part, :], in0=ada_raw[part][:, :],
                                             scalar=c_silu[:, bass.ds(i * 2 + k, 1)],
                                             in1=ada_acc[:, part, :], op0=ALU.mult, op1=ALU.add
                                             ).then_inc(ada_used, 1)

            def ada_first(t):
                part, k = FIRST_PARTS[t // DT], t % DT
                dve.wait_ge(ada_full[t % 3], 16 * (t // 3 + 1))
                if t:
                    dve.wait_ge(ada_used, t)
                if k == 0:
                    dve.tensor_scalar(ada_acc[:, part, :], ada_raw[t % 3][:, :], c_silu[:, 0:1], None,
                                      ALU.mult).then_inc(ada_used, 1)
                else:
                    dve.scalar_tensor_tensor(out=ada_acc[:, part, :], in0=ada_raw[t % 3][:, :],
                                             scalar=c_silu[:, k:k + 1], in1=ada_acc[:, part, :],
                                             op0=ALU.mult, op1=ALU.add).then_inc(ada_used, 1)

            def ada_next(m, count):
                for _ in range(count):
                    ada_block(m, ada_at[0] // 3, ada_at[0] % 3)
                    ada_at[0] += 1

            def modulation(m, name=None, cols=slice(0, 3 * DT)):
                name = name or f"mod{m}"
                src = bank_full(dve, name)
                b = V_ADAB + 3 * DT * m
                bank_read(name, dve.tensor_tensor(MOD[:, m, cols], src[:, cols],
                                                  V[:, b + cols.start:b + cols.stop], ALU.add))
                bank_was_read(dve, name)
                if cols.start:
                    return
                dve.scalar_tensor_tensor(out=GAIN[:, m, :], in0=MOD[:, m, DT:2 * DT], scalar=1.0,
                                         in1=V[:, DT * m:DT * (m + 1)], op0=ALU.add, op1=ALU.mult
                                         ).then_inc(mod_ready, 1)
                dve.wait_ge(mod_ready, m + 1)

            ssq = [0]

            def add_squares(t, first):
                into = sq_sum if first else sq
                ins = dve.tensor_tensor(into[:, :, :], X[:, t:t + 2, :], X[:, t:t + 2, :], ALU.mult)
                if not first:
                    chain(ins)
                    ins = dve.tensor_tensor(sq_sum[:, :, :], sq_sum[:, :, :], sq[:, :, :], ALU.add)
                ins.then_inc(ssq_ready, 1)
                ssq[0] += 1
                dve.wait_ge(ssq_ready, ssq[0])

            def residual_pair(n, u, t, gate):
                dve.wait_ge(block_used, n + 1)
                src = halves(G[u % 4])
                if gate is None:
                    ins = dve.tensor_tensor(X[:, t:t + 2, :], src, X[:, t:t + 2, :], ALU.add)
                else:
                    for m in range(2):
                        ins = dve.scalar_tensor_tensor(out=X[:, t + m, :], in0=src[:, m, :],
                                                       scalar=gate[:, t + m:t + m + 1], in1=X[:, t + m, :],
                                                       op0=ALU.mult, op1=ALU.add)
                ins.then_inc(g_free[u % 4], 1)
                dve.wait_ge(g_free[u % 4], u // 4 + 1)
                add_squares(t, t == 0)

            def clear_sums():
                dve.memset(sq_sum[:, 0, :], 0.0).then_inc(down_free0, 1)
                dve.memset(sq_sum[:, 1, :], 0.0).then_inc(down_free1, 1)

            def residual_tile(phase, n, g, m, gate, i=0):
                if m == 0:
                    dve.wait_ge(down_half, 4 * phase + g + 1 + i)
                else:
                    dve.wait_ge(block_used, n + 1 + i * 4)
                at = i * 2 + (2 * g + m)
                xt = X[:, bass.ds(at, 1), :].rearrange("p a s -> p (a s)")
                if gate is None:
                    ins = dve.tensor_tensor(xt, A[m][:, 0:S], xt, ALU.add)
                else:
                    ins = dve.scalar_tensor_tensor(out=xt, in0=A[m][:, 0:S], scalar=gate[:, bass.ds(at, 1)],
                                                   in1=xt, op0=ALU.mult, op1=ALU.add)
                free = (down_free0, down_free1)[m]
                ins.then_inc(free, 1)
                dve.wait_ge(free, 5 * phase + g + 2 + i)
                chain(dve.tensor_tensor(sq[:, m, :], xt, xt, ALU.mult))
                dve.tensor_tensor(sq_sum[:, m, :], sq_sum[:, m, :], sq[:, m, :], ALU.add
                                  ).then_inc(ssq_ready, 1)

            def low_pair(split, p, src, position=None, shift=None):
                position = p if position is None else position
                dve.wait_ge(hhi_ready, 4 * SPLIT[split] + position + 1)
                hi = h_hi[:, 2 * p:2 * p + 2, :].bitcast(F32)
                if shift is None:
                    ins = dve.tensor_tensor(h_lo[:, 2 * p:2 * p + 2, :], src, hi, ALU.subtract)
                else:
                    for m in range(2):
                        ins = dve.scalar_tensor_tensor(out=h_lo[:, 2 * p + m, :], in0=src[:, m, :],
                                                       scalar=shift[:, 2 * p + m:2 * p + m + 1],
                                                       in1=hi[:, m, :], op0=ALU.add, op1=ALU.subtract)
                ins.then_inc(h_ready, 1)

            def norm(split, k, gain, shift=None):
                dve.wait_ge(rstd_ready, k + 1)
                for p in range(5):
                    if p < 4:
                        if p >= 2:
                            dve.wait_ge(h_ready, 4 * SPLIT[split] + p - 1)
                        for m in range(2):
                            t = 2 * p + m
                            ins = dve.scalar_tensor_tensor(out=HN[p % 2][:, m, :], in0=X[:, t, :],
                                                           scalar=gain[:, t:t + 1], in1=rstd[:, :],
                                                           op0=ALU.mult, op1=ALU.mult)
                        ins.then_inc(norm_ready, 1)
                    if p >= 1:
                        dve.wait_ge(norm_ready, 4 * NORMED[split] + p)
                        low_pair(split, p - 1, HN[(p - 1) % 2][:, :, :], shift=shift)

            def norm_in_place(k, gain):
                dve.wait_ge(rstd_ready, k + 1)
                for t in range(DT):
                    ins = dve.scalar_tensor_tensor(out=X[:, t, :], in0=X[:, t, :], scalar=gain[:, t:t + 1],
                                                   in1=rstd[:, :], op0=ALU.mult, op1=ALU.mult)
                return ins

            def biased(r, v):
                hp, b = v // 2, v % 2
                keys = S if b else P
                src = halves(bank_full(dve, f"scores{r}{v}"))
                s = SS[:, v % 2, :, 0:keys]
                bank_read(f"scores{r}{v}",
                          dve.tensor_tensor(s, src[:, :, 0:keys],
                                            BIAS[:, 2 * hp:2 * hp + 2, S - keys:S], ALU.add))
                bank_was_read(dve, f"scores{r}{v}")
                mx, nm = stat[:, v % 2, 0:2], stat[:, v % 2, 2:4]
                chain(dve.tensor_reduce(mx, s, AX_X, ALU.max))
                if r == 0:
                    chain(dve.tensor_tensor(mx, mx, sinks[:, 2 * hp:2 * hp + 2], ALU.max))
                dve.tensor_scalar(nm, mx, -1.0, None, ALU.mult).then_inc(max_ready, 1)

            def scaled(r, v):
                keys = S if v % 2 else P
                dve.wait_ge(prob_ready, ATT_UNITS * r + v + 1)
                total, es = stat[:, v % 2, 4:6], stat[:, v % 2, 6:8]
                if r == 0:
                    chain(dve.tensor_tensor(total, total, es, ALU.add))
                chain(dve.reciprocal(total, total))
                for e in range(2):
                    pr = PR[:, v % 2, e, 0:keys]
                    ins = dve.tensor_scalar(pr, pr, total[:, e:e + 1], None, ALU.mult)
                ins.then_inc(prob_scaled, 1)

            def attended(r, v):
                t, b = v // 2 + (0 if r else 4), v % 2
                src = bank_full(dve, f"att_out{r}{v}")
                bank_read(f"att_out{r}{v}", dve.tensor_copy(MIX[:, t, b * P:b * P + P], src[:, 0:P]))

            def attention(r, v, n):
                if v < ATT_UNITS:
                    biased(r, v)
                split_lo(n)
                if v >= 2:
                    attended(r, v - 2)
                if v < ATT_UNITS:
                    scaled(r, v)

            dve.memset(ones[:, :], 1.0)
            dve.memset(eps6[:, :], EPS)
            dve.memset(eps5[:, :], GN_EPS)
            dve.memset(one[:, :], 1.0)
            dve.memset(reset[:, :], 1.0)
            dve.memset(ST[:, :, :, :], 0.0)
            dve.memset(t8[:, :], NEG).then_inc(setup_ready, 1)
            dve.wait_ge(setup_ready, 1)
            chain(dve.memset(reset[:, :].rearrange("p (c j) -> p c j", j=64)[:, :, 0:1], 0.0))
            src = bank_full(dve, "vecs")
            bank_read("vecs", dve.tensor_copy(V[:, :], src[:, 0:V_ALL]))
            src = bank_full(dve, "table")
            bank_read("table", dve.tensor_copy(t8[:, P:2 * P], src[0:HEADS, 0:P]))
            bank_was_read(dve, "vecs")
            dve.wait_ge(c_sigmoid, 1)
            chain(dve.tensor_tensor(c_silu[:, :], c_tmp[:, :], V[:, V_C:V_C + DT], ALU.mult))
            for q in range(4):
                bank_was_read(dve, f"x{q}")
                add_squares(2 * q, q == 0)
            for t in range(2 * DT):
                ada_first(t)
                if t == DT:
                    dve.wait_ge(g_split, 1)
                    dve.tensor_tensor(g_lo[:, :, :], g_raw[:, :, :], g_hi[:, :, :].bitcast(F32),
                                      ALU.subtract).then_inc(g_ready, 1)
                    split_lo(0)
            modulation(0, cols=slice(0, 2 * DT))
            norm("n0", 0, GAIN[:, 0, :], MOD[:, 0, 0:DT])
            split_lo(1)

            split_lo(2)
            dve.wait_ge(block_used, 1)
            dve.tensor_copy(K4[:, 0, :], G[0][:, 0:S])
            dve.tensor_copy(K4[64:128, 1, :], G[0][0:64, 0:S])
            dve.tensor_copy(K4[0:64, 1, :], G[0][64:128, 0:S])
            dve.tensor_copy(V4[:, :, 0:P], G[0][:, S:2 * S].rearrange("p (k f) -> p k f", k=2)
                            ).then_inc(g_free[0], 1)
            for t in (16, 17):
                ada_first(t)
            src = bank_full(dve, "glr")
            bank_read("glr", dve.tensor_copy(GLT[:, :, :], src[:, 0:32].rearrange("p (k r) -> p k r", k=2)))
            for q in range(4):
                bank_was_read(dve, f"flip{q}")
            dve.wait_ge(small_in, 48)
            attention(0, 0, 3)
            for t in (18, 19):
                ada_first(t)
            src = bank_full(dve, "glt")
            bank_read("glt", dve.tensor_copy(GL[:, :], src[0:16, 0:S]))
            attention(0, 1, 4)
            for t in (20, 21):
                ada_first(t)
            attention(0, 2, 5)
            for t in (22, 23):
                ada_first(t)
            attention(0, 3, 6)
            dve.wait_ge(z_ready, 1)
            chain(dve.scalar_tensor_tensor(out=GZ, in0=GZ, scalar=0.0, in1=GA, op0=ALU.min,
                                           op1=ALU.subtract))
            chain(dve.tensor_scalar(GZ, GZ, 1.0 / 16.0, None, ALU.mult))
            dve.tensor_tensor_scan(wide[:, 4, :], reset[:, :], wide[:, 2, :], 0.0, ALU.mult, ALU.add
                                   ).then_inc(decay_ready, 1)
            modulation(0, "gate0", slice(2 * DT, 3 * DT))
            attention(0, 4, 7)
            ada_next(1, 3)
            attention(0, 5, 8)
            dve.wait_ge(exp_ready, 1)
            dve.tensor_tensor(GQ, GQ, EB, ALU.mult)
            dve.tensor_tensor(KE, GK, KE, ALU.mult)
            dve.tensor_tensor(GK, GK, ENB, ALU.mult).then_inc(gla_ready, 1)
            ada_next(1, 3)
            attention(0, 6, 9)
            bank_was_read(dve, "kend")
            chain(dve.memset(AM, 0.0))
            for k in range(2):
                src = bank_full(dve, f"gs{k}")
                bank_read(f"gs{k}", dve.copy_predicated(AM[:, k, :, :], spread(chunk_mask, 4),
                                                        src[:, :].rearrange("p (h s) -> p h s", h=4)))
            ada_next(1, 2)
            attention(0, 7, 10)
            def increments(name, at, m, ch):
                src = bank_full(dve, name)
                for e in range(2):
                    half = slice(64 * e, 64 * e + 64)
                    inc = src[half, at + e * P:at + e * P + P]
                    if ch == 0:
                        ins = dve.tensor_copy(ST[half, 2 * m + e, 0, :], inc)
                    else:
                        ins = dve.scalar_tensor_tensor(out=ST[half, 2 * m + e, ch, :],
                                                       in0=ST[half, 2 * m + e, ch - 1, :],
                                                       scalar=EB[half, m, ch * 64 + 63:ch * 64 + 64],
                                                       in1=inc, op0=ALU.mult, op1=ALU.add)
                return ins

            for m in range(2):
                chain(increments(f"ds{m}", 0, m, 0))
            for m in range(2):
                bank_read(f"ds{m}", increments(f"ds{m}", S, m, 1))
                bank_was_read(dve, f"ds{m}")
            attended(0, 6)
            increments("ds2", 0, 0, 2)
            bank_read("ds2", increments("ds2", S, 1, 2))
            attended(0, 7)
            ada_next(1, 4)
            for a, p in enumerate((2, 3)):
                low_pair("mix0", p, MIX[:, 2 * p:2 * p + 2, :], position=a)
            for m in range(2):
                dve.wait_ge(g_free[(3, 0)[m]], (2, 3)[m])
                chain(dve.tensor_tensor(GG[:, 2 * m:2 * m + 2, :], GG[:, 2 * m:2 * m + 2, :],
                                        GE[:, 2 * m:2 * m + 2, :], ALU.mult))
            for m in range(2):
                bank_was_read(dve, f"go{m}")
                o = O[:, 2 * m:2 * m + 2, :]
                dve.tensor_tensor(OSQ[:, 2 * m:2 * m + 2, :], o, o, ALU.mult).then_inc(osq_ready, 1)
            for m in range(2):
                dve.wait_ge(ors_ready, m + 1)
                mix = MIX[:, 2 * m:2 * m + 2, :]
                chain(dve.scalar_tensor_tensor(out=mix, in0=O[:, 2 * m:2 * m + 2, :],
                                               scalar=V[:, V_GLAW:V_GLAW + 1],
                                               in1=RO[:, 2 * m:2 * m + 2, :], op0=ALU.mult, op1=ALU.mult))
                dve.tensor_tensor(mix, mix, GG[:, 2 * m:2 * m + 2, :], ALU.mult).then_inc(mix_ready, 1)
                dve.wait_ge(mix_ready, m + 1)
            for m in range(2):
                low_pair("mix0", m, MIX[:, 2 * m:2 * m + 2, :], position=2 + m)
            for j in range(3):
                split_lo(N_OUT + j + 2)
                ada_next(1, 4)
                residual_pair(N_OUT + j, 9 + j, 2 * j, MOD[:, 0, 2 * DT:])
            residual_pair(N_OUT + 3, 12, 6, MOD[:, 0, 2 * DT:])
            modulation(1)
            norm("n1", 1, GAIN[:, 1, :], MOD[:, 1, 0:DT])
            split_lo(N_OUT + 5)

            def mlp(layer):
                with_ada = layer == 0
                start = chain.count
                if with_ada:
                    dve.wait_ge(acc_clear, 1)
                with dve.Fori(0, 4) as i:
                    chain.looped = i * 4
                    done = 0
                    for j in range(4):
                        split_lo(N_UP[layer] + j + 2, i)
                        for _ in range((2, 1, 2, 1)[j] if with_ada else 0):
                            ada_block(2, done // 3, done % 3, i)
                            done += 1
                        dve.wait_ge(uhi_ready, 16 * layer + j + 1 + i * 4)
                        chain(dve.tensor_tensor(relu[j % 2][:, :, :], relu[j % 2][:, :, :],
                                                relu[j % 2][:, :, :], ALU.mult))
                        at = bass.ds(i * 8 + 2 * j, 2)
                        dve.tensor_tensor(u_lo[:, at, :], relu[j % 2][:, :, :], u_hi[:, at, :].bitcast(F32),
                                          ALU.subtract).then_inc(u_ready, 1)
                chain.looped, chain.count = 0, start + 16
                clear_sums()
                if with_ada:
                    modulation(2)
                    dve.wait_ge(acc_clear, 2)
                start = chain.count
                with dve.Fori(0, 4) as i:
                    chain.looped = i * 2
                    done = 0
                    for j in range(4):
                        n = N_DOWN[layer] + j
                        if j < 3:
                            split_lo(n + 2, i)
                        for _ in range((2, 2, 2, 0)[j] if with_ada else 0):
                            ada_block(3, done // 3, done % 3, i)
                            done += 1
                    for m in range(2):
                        residual_tile(layer, n, 0, m, MOD[:, 1 + 2 * layer, 2 * DT:], i)
                    split_lo(n + 2, i)
                chain.looped, chain.count = 0, start + 8
                ssq[0] += 8

            mlp(0)

            dve.wait_ge(rstd_ready, 3)
            for buf in (*pad, win):
                ins = dve.memset(buf[:, :, 0:POOL_PAD], 0.0)
            H = pad[0]
            for t in range(DT):
                ins = dve.scalar_tensor_tensor(out=H[:, t, POOL_PAD:], in0=X[:, t, :],
                                               scalar=GAIN[:, 2, t:t + 1], in1=rstd[:, :],
                                               op0=ALU.mult, op1=ALU.mult)
            chain(ins)
            for t in range(DT):
                ins = dve.tensor_scalar(H[:, t, POOL_PAD:], H[:, t, POOL_PAD:], MOD[:, 2, t:t + 1], None,
                                        ALU.add)
            chain(ins)
            chain(dve.tensor_tensor(gate_ps[:, :], MOD[:, 2, 2 * DT:], V[:, V_PSCALE:V_PSCALE + DT], ALU.mult))
            sums, src = (pad[1], win, pad[1], win), H
            for g in range(4):
                back = 1 << g
                chain(dve.tensor_tensor(sums[g][:, 2 * g:, POOL_PAD:], src[:, 2 * g:, POOL_PAD:],
                                        src[:, 2 * g:, POOL_PAD - back:POOL_PAD + S - back], ALU.add))
                src = sums[g]
            for g in range(5):
                if g < 4:
                    if g >= 2:
                        dve.wait_ge(h_ready, 4 * SPLIT["pool"] + g - 1)
                    tiles = slice(2 * g, 2 * g + 2)
                    hn, head = HN[g % 2], sums[g][:, tiles, POOL_PAD:2 * POOL_PAD]
                    count = spread(C[:, C_CNT_AT + g * POOL_PAD:C_CNT_AT + (g + 1) * POOL_PAD], 2)
                    chain(dve.tensor_tensor(head, head, count, ALU.mult))
                    dve.scalar_tensor_tensor(out=hn[:, :, POOL_PAD:], in0=sums[g][:, tiles, 2 * POOL_PAD:],
                                             scalar=1.0 / (2 << g), in1=H[:, tiles, 2 * POOL_PAD:],
                                             op0=ALU.mult, op1=ALU.subtract)
                    dve.tensor_tensor(hn[:, :, 0:POOL_PAD], head, H[:, tiles, POOL_PAD:2 * POOL_PAD],
                                      ALU.subtract).then_inc(norm_ready, 1)
                if g >= 1:
                    dve.wait_ge(norm_ready, 4 * NORMED["pool"] + g)
                    low_pair("pool", g - 1, HN[(g - 1) % 2][:, :, :])
            for g in range(4):
                residual_pair(N_POOL, U_POOL + g, 2 * g, gate_ps)
            modulation(3)
            norm("n3", 3, GAIN[:, 3, :], MOD[:, 3, 0:DT])
            split_lo(N_POOL + 2)
            mlp(1)
            chain(norm_in_place(4, V[:, V_FINAL:V_FINAL + DT]))
            for t in range(0, DT, 2):
                add_squares(t, t == 0)
            norm("n5", 5, V[:, V_ATTN2:V_ATTN2 + DT])

            for h in range(HEADS):
                ins = dve.tensor_scalar(BIAS[:, h, :], C[:, C_DIST:C_DIST + S], 2.0 ** -(h + 1), None,
                                        ALU.mult)
            chain(ins)
            for j in range(3):
                split_lo(N_IN2 + j + 2)
            for j in range(3, 13):
                attention(1, j - 3, N_IN2 + j + 2)
            split_lo(N_IN2 + 15)
            dve.wait_ge(decay_in, 16)
            for h in range(4):
                src = bank_full(dve, f"rs{h}")
                dve.tensor_tensor(RS[h][:, 0:S], src[:, 0:S], DECAY[:, h, :], ALU.mult)
                bank_read(f"rs{h}", dve.tensor_tensor(RS[h][:, S:S + P], src[:, S:S + P], DECAY[:, h, 0:P],
                                                      ALU.mult))
            for p in range(2):
                low_pair("mix1", p, MIX[:, 2 * p:2 * p + 2, :])
            for m in range(2):
                u = U_IN2 + 12 + m
                dve.wait_ge(g_free[u % 4], u // 4 + 1)
                chain(dve.tensor_tensor(RG[:, 2 * m:2 * m + 2, :], RG[:, 2 * m:2 * m + 2, :],
                                        RT[:, 2 * m:2 * m + 2, :], ALU.mult))
            for m in range(2):
                src = bank_full(dve, f"rm{m}")
                o = GG[:, 2 * m:2 * m + 2, :]
                bank_read(f"rm{m}", dve.scalar_tensor_tensor(out=o, in0=halves(src), scalar=-1.0 / P, in1=o,
                                                             op0=ALU.mult, op1=ALU.add))
                bank_was_read(dve, f"rm{m}")
                dve.tensor_tensor(OSQ[:, 2 * m:2 * m + 2, :], o, o, ALU.mult).then_inc(osq_ready, 1)
            for m in range(2):
                dve.wait_ge(ors_ready, 2 + m + 1)
                mix = MIX[:, 4 + 2 * m:6 + 2 * m, :]
                for e in range(2):
                    h = 2 * m + e
                    ins = dve.scalar_tensor_tensor(out=MIX[:, 4 + h, :], in0=GG[:, h, :],
                                                   scalar=V[:, V_RET + h:V_RET + h + 1], in1=RO[:, h, :],
                                                   op0=ALU.mult, op1=ALU.mult)
                chain(ins)
                dve.tensor_tensor(mix, mix, RG[:, 2 * m:2 * m + 2, :], ALU.mult).then_inc(mix_ready, 1)
                dve.wait_ge(mix_ready, 2 + m + 1)
            for m in range(2):
                low_pair("mix1", 2 + m, MIX[:, 4 + 2 * m:6 + 2 * m, :])
            for j in range(3):
                split_lo(N_OUT2 + j + 2)
                residual_pair(N_OUT2 + j, U_OUT2 + j, 2 * j, None)
            residual_pair(N_OUT2 + 3, U_OUT2 + 3, 6, None)
            norm("n6", 6, V[:, V_FFN2:V_FFN2 + DT])
            dve.memset(UP[:, :, 0:2], 0.0).then_inc(pads_ready, 1)
            split_lo(N_OUT2 + 5)

            def gated_up(j, i=0):
                u = U_FFN + j
                dve.wait_ge(g_free[u % 4], u // 4 + 1 + i)
                def vec(base, m):
                    return V[:, bass.ds(i * 4 + (base + 2 * (j // 2) + m), 1)] if j < 20 else \
                        V[:, base + 20 + m:base + 21 + m]
                for m in range(2):
                    ins = dve.tensor_scalar(CV[:, m, :], UP[:, m, 2:], vec(V_CONVW + 2 * F2T, m),
                                            vec(V_CONVB, m), ALU.mult, ALU.add)
                chain(ins)
                for tap in (1, 0):
                    for m in range(2):
                        ins = dve.scalar_tensor_tensor(out=CV[:, m, :], in0=UP[:, m, tap:tap + S],
                                                       scalar=vec(V_CONVW + tap * F2T, m), in1=CV[:, m, :],
                                                       op0=ALU.mult, op1=ALU.add)
                    if tap:
                        chain(ins)
                ins.then_inc(conv_ready, 1)

            def gated_gate(j, i=0):
                u, p = U_FFN + j, j // 2
                dve.wait_ge(gelu_ready, p + 1 + i * 2)
                dve.wait_ge(block_used, N_FFN + j + 1 + i * 4)
                dve.tensor_tensor(GU[:, :, :], halves(G[u % 4]), GU[:, :, :], ALU.mult
                                  ).then_inc(g_free[u % 4], 1)
                dve.wait_ge(fhi_ready, p + 1 + i * 2)
                at = bass.ds(i * 4 + 2 * p, 2) if j < 20 else slice(20, 22)
                dve.tensor_tensor(f_lo[:, at, :], GU[:, :, :], f_hi[:, at, :].bitcast(F32), ALU.subtract
                                  ).then_inc(f_ready, 1)

            start = chain.count
            with dve.Fori(0, 5) as i:
                chain.looped = i * 4
                for j in range(4):
                    split_lo(N_FFN + j + 2, i)
                    (gated_gate if j % 2 else gated_up)(j, i)
            chain.looped, chain.count = 0, start + 20
            for j in (20, 21):
                split_lo(N_FFN + j + 2)
                (gated_gate if j % 2 else gated_up)(j)
            clear_sums()
            for g in range(4):
                for j in range(3):
                    if j < 2:
                        split_lo(N_FDOWN + 3 * g + j + 2)
                for m in range(2):
                    residual_tile(2, N_FDOWN + 3 * g + 2, g, m, None)
                    ssq[0] += 1
                split_lo(N_FDOWN + 3 * g + 4)
            norm("n7", 7, V[:, V_PLE2:V_PLE2 + DT])
            dve.wait_ge(phi_ready, 1)
            dve.tensor_tensor(p_lo[:, :, :], p_t[:, :, :], p_hi[:, :, :].bitcast(F32), ALU.subtract
                              ).then_inc(p_ready, 1)
            split_lo(N_PLE + 2)
            for j in range(4):
                if j < 2:
                    split_lo(N_PLEG + j + 2)
                u = U_PLEG + j
                dve.wait_ge(g_free[u % 4], u // 4 + 1)
                chain(dve.tensor_tensor(SG[:, :, :], SG[:, :, :], PE8[:, 2 * j:2 * j + 2, :], ALU.mult))
                chain(dve.tensor_tensor(X[:, 2 * j:2 * j + 2, :], X[:, 2 * j:2 * j + 2, :], SG[:, :, :],
                                        ALU.add))
                add_squares(2 * j, j == 0)
            norm_in_place(8, V[:, V_FINAL2:V_FINAL2 + DT]).then_inc(fin_ready, 1)

        @block.scalar
        def _(act):
            chain = Chain(act, act_step)

            def split_hi(n, i=0):
                k = k_tiles(n)
                act.wait_ge(raw_full[n % RAW], 16 * (n // RAW + 1) + i * 16)
                if n >= 2:
                    act.wait_ge(block_used, n - 1 + i * 4)
                act.activation(w_hi[n % 2][:, 0:k, :], raw[n % RAW][:, 0:k, :], ACT.Copy
                               ).then_inc(hi_done, 1)

            def root(norm):
                src = bank_full(act, f"ms{norm}")
                bank_read(f"ms{norm}", act.activation(ln_ms[:, :], src[:, 0:S], ACT.Ln, bias=eps6[:, 0:1],
                                                      scale=1.0 / D))
                bank_was_read(act, f"ms{norm}")
                act.activation(rstd[:, :], ln_ms[:, :], ACT.Exp, scale=-0.5).then_inc(rstd_ready, 1)

            def high_norm(split, shift=None):
                for p in range(4):
                    act.wait_ge(norm_ready, 4 * NORMED[split] + p + 1)
                    src = HN[p % 2]
                    if shift is None:
                        ins = act.activation(h_hi[:, 2 * p:2 * p + 2, :], src[:, :, :], ACT.Copy)
                    else:
                        for m in range(2):
                            t = 2 * p + m
                            ins = act.activation(h_hi[:, t, :], src[:, m, :], ACT.Identity,
                                                 bias=shift[:, t:t + 1])
                    ins.then_inc(hhi_ready, 1)

            def high_mix(p):
                act.activation(h_hi[:, 2 * p:2 * p + 2, :], MIX[:, 2 * p:2 * p + 2, :], ACT.Copy
                               ).then_inc(hhi_ready, 1)

            def leave(n, u, dst, scale=1.0):
                act.wait_ge(block_used, n + 1)
                act.activation(dst, halves(G[u % 4]), ACT.Copy, scale=scale).then_inc(g_free[u % 4], 1)

            def silu_parts(n, u, sigmoid, plain):
                act.wait_ge(block_used, n + 1)
                act.activation(plain, halves(G[u % 4]), ACT.Copy)
                act.activation(sigmoid, halves(G[u % 4]), ACT.Sigmoid).then_inc(g_free[u % 4], 1)

            def attention(r, v):
                if 1 <= v <= ATT_UNITS:
                    w = v - 1
                    src = bank_full(act, f"turned{r}{w}")
                    dst = PT[:, w % 2, :, :].rearrange("p (e k) s -> p e k s", e=2)[:, :, 0:w % 2 + 1, :]
                    bank_read(f"turned{r}{w}", act.activation(
                        dst, src[:, :].rearrange("p (e k s) -> p e k s", e=2, k=2)[:, :, 0:w % 2 + 1, :],
                        ACT.Copy))
                if v < ATT_UNITS:
                    hp, keys = v // 2, S if v % 2 else P
                    act.wait_ge(max_ready, ATT_UNITS * r + v + 1)
                    for e in range(2):
                        nm = stat[:, v % 2, 2 + e:3 + e]
                        if r == 0:
                            h = 2 * hp + e
                            act.activation(stat[:, v % 2, 6 + e:7 + e], sinks[:, h:h + 1], ACT.Exp, bias=nm)
                        ins = act.activation(PR[:, v % 2, e, 0:keys], SS[:, v % 2, e, 0:keys], ACT.Exp,
                                             bias=nm, accum_out=stat[:, v % 2, 4 + e:5 + e])
                    ins.then_inc(prob_ready, 1)

            def head_roots(names, eps):
                for m, name in enumerate(names):
                    src = bank_full(act, name)
                    ro = RO[:, 2 * m:2 * m + 2, :]
                    bank_read(name, act.activation(ro, halves(src), ACT.Ln, bias=eps[:, 0:1], scale=1.0 / P))
                    bank_was_read(act, name)
                    act.activation(ro, ro, ACT.Exp, scale=-0.5).then_inc(ors_ready, 1)

            bank_was_read(act, "vecs")
            act.activation(c_tmp[:, :], V[:, V_C:V_C + DT], ACT.Sigmoid).then_inc(c_sigmoid, 1)
            for q in range(4):
                src = bank_full(act, f"x{q}")
                bank_read(f"x{q}", act.activation(X[:, 2 * q:2 * q + 2, :], halves(src), ACT.Copy))
            act.wait_ge(glr_in, 16)
            act.activation(g_hi[:, :, :], g_raw[:, :, :], ACT.Copy).then_inc(g_split, 1)
            for q in range(4):
                src = bank_full(act, f"flip{q}")
                bank_read(f"flip{q}", act.activation(BIAS[:, 2 * q:2 * q + 2, :], halves(src), ACT.Copy))
            split_hi(0)
            root(0)
            act.wait_ge(mod_ready, 1)
            high_norm("n0", MOD[:, 0, 0:DT])
            split_hi(1)

            split_hi(2)
            leave(1, 1, Q4[:, 0:2, :], 0.125)
            split_hi(3)
            attention(0, 0)
            leave(2, 2, Q4[:, 2:4, :], 0.125)
            split_hi(4)
            attention(0, 1)
            leave(3, 3, GQ, 0.125)
            split_hi(5)
            src = bank_full(act, "logits")
            for m in range(2):
                act.activation(GZ[:, m, :], halves(src)[:, m, :], ACT.Identity,
                               bias=V[:, V_BGATE + m:V_BGATE + m + 1])
            for m in range(2):
                ins = act.activation(GA[:, m, :], halves(src)[:, m, :], ACT.Abs,
                                     bias=V[:, V_BGATE + m:V_BGATE + m + 1])
            bank_read("logits", ins)
            attention(0, 2)
            bank_was_read(act, "logits")
            chain(act.activation(GA, GA, ACT.Exp, scale=-1.0))
            act.activation(GA, GA, ACT.Ln, bias=one[:, 0:1]).then_inc(z_ready, 1)
            leave(4, 4, GK)
            split_hi(6)
            attention(0, 3)
            leave(5, 5, GV[:, :, 0:S])
            split_hi(7)
            attention(0, 4)
            act.wait_ge(decay_ready, 1)
            act.activation(EB, GB, ACT.Exp)
            act.activation(ENB, GB, ACT.Exp, scale=-1.0)
            for m in range(2):
                for ch in range(4):
                    toks = slice(ch * 64, ch * 64 + 64)
                    ins = act.activation(KE[:, m, toks], GB[:, m, toks], ACT.Exp, scale=-1.0,
                                         bias=GB[:, m, ch * 64 + 63:ch * 64 + 64])
            ins.then_inc(exp_ready, 1)
            leave(6, 6, GV[:, :, S:2 * S])
            split_hi(8)
            attention(0, 5)
            act.wait_ge(block_used, 8)
            split_hi(9)
            src = bank_full(act, "kend")
            bank_read("kend", act.activation(KET, src[:, :].rearrange("p (a s) -> p a s", a=4), ACT.Copy))
            attention(0, 6)
            split_hi(10)
            attention(0, 7)
            silu_parts(7, 7, GE[:, 0:2, :], GG[:, 0:2, :])
            silu_parts(8, 8, GE[:, 2:4, :], GG[:, 2:4, :])
            attention(0, 8)
            bank_was_read(act, "att_out07")
            for p in (2, 3):
                high_mix(p)
            for m in range(2):
                src = bank_full(act, f"go{m}")
                bank_read(f"go{m}", act.activation(O[:, 2 * m:2 * m + 2, :], halves(src), ACT.Copy))
            head_roots(("gm0", "gm1"), eps6)
            for m in range(2):
                act.wait_ge(mix_ready, m + 1)
                high_mix(m)
            for j in range(4):
                split_hi(N_OUT + j + 2)
            root(1)
            act.wait_ge(mod_ready, 2)
            high_norm("n1", MOD[:, 1, 0:DT])

            def mlp(layer):
                with act.Fori(0, 4) as i:
                    for j in range(4):
                        n, u = N_UP[layer] + j, U_UP[layer] + j
                        split_hi(n + 2, i)
                        act.wait_ge(block_used, n + 1 + i * 4)
                        act.wait_ge(lo_done, n + 2 + i * 4)
                        act.activation(relu[j % 2][:, :, :], halves(G[u % 4]), ACT.Relu
                                       ).then_inc(g_free[u % 4], 1)
                        act.wait_ge(g_free[u % 4], u // 4 + 1 + i)
                        act.activation(u_hi[:, bass.ds(i * 8 + 2 * j, 2), :], relu[j % 2][:, :, :],
                                       ACT.Square).then_inc(uhi_ready, 1)
                with act.Fori(0, 4) as i:
                    for j in range(4):
                        split_hi(N_DOWN[layer] + j + 2, i)

            mlp(0)
            root(2)
            for g in range(4):
                act.wait_ge(norm_ready, 4 * NORMED["pool"] + g + 1)
                act.activation(h_hi[:, 2 * g:2 * g + 2, :], HN[g % 2][:, :, :], ACT.Copy
                               ).then_inc(hhi_ready, 1)
            split_hi(N_POOL + 2)
            root(3)
            act.wait_ge(mod_ready, 4)
            high_norm("n3", MOD[:, 3, 0:DT])
            mlp(1)
            root(4)
            root(5)
            high_norm("n5")

            outs = [(Q4[:, 0:2, :], 0.125), (Q4[:, 2:4, :], 0.125), (K4[:, 0:2, :], 1.0),
                    (K4[:, 2:4, :], 1.0), (V4[:, :, 0:S], 1.0), (V4[:, :, S:2 * S], 1.0),
                    (RQ[:, 0:2, :], 1.0), (RQ[:, 2:4, :], 1.0), (RK[:, 0:2, :], 128 ** -0.5),
                    (RK[:, 2:4, :], 128 ** -0.5), (V4r[:, :, 0:S], 1.0), (V4r[:, :, S:2 * S], 1.0)]
            for j in range(14):
                if j < 12:
                    leave(N_IN2 + j, U_IN2 + j, *outs[j])
                split_hi(N_IN2 + j + 2)
                if j >= 12:
                    a = 2 * (j - 12)
                    silu_parts(N_IN2 + j, U_IN2 + j, RT[:, a:a + 2, :], RG[:, a:a + 2, :])
                if 3 <= j < 12:
                    attention(1, j - 3)
            bank_was_read(act, "att_out17")
            for p in range(2):
                high_mix(p)
            for m in range(2):
                src = bank_full(act, f"ro{m}")
                bank_read(f"ro{m}", act.activation(GG[:, 2 * m:2 * m + 2, :], halves(src), ACT.Copy))
            head_roots(("rv0", "rv1"), eps5)
            for m in range(2):
                act.wait_ge(mix_ready, 2 + m + 1)
                high_mix(2 + m)
            for j in range(4):
                split_hi(N_OUT2 + j + 2)
            root(6)
            high_norm("n6")

            def gated_up(j, i=0):
                u, p = U_FFN + j, j // 2
                act.wait_ge(block_used, N_FFN + j + 1 + i * 4)
                act.activation(UP[:, :, 2:], halves(G[u % 4]), ACT.Copy).then_inc(g_free[u % 4], 1)

            def gated_gate(j, i=0):
                u, p = U_FFN + j, j // 2
                act.wait_ge(conv_ready, p + 1 + i * 2)
                act.activation(GU[:, :, :], CV[:, :, :], ACT.Gelu_apprx_tanh).then_inc(gelu_ready, 1)
                act.wait_ge(g_free[u % 4], u // 4 + 1 + i)
                at = bass.ds(i * 4 + 2 * p, 2) if j < 20 else slice(20, 22)
                act.activation(f_hi[:, at, :], GU[:, :, :], ACT.Copy).then_inc(fhi_ready, 1)

            act.wait_ge(pads_ready, 1)
            with act.Fori(0, 5) as i:
                for j in range(4):
                    split_hi(N_FFN + j + 2, i)
                    if j % 2:
                        gated_gate(j, i)
                    else:
                        gated_up(j, i)
            split_hi(N_FFN + 22)
            gated_up(20)
            split_hi(N_FFN + 23)
            gated_gate(21)
            for g in range(4):
                for j in range(3):
                    split_hi(N_FDOWN + 3 * g + j + 2)
            root(7)
            high_norm("n7")
            src = bank_full(act, "pt")
            bank_read("pt", act.activation(p_t[:, :, :], halves(src), ACT.Copy))
            bank_was_read(act, "pt")
            act.activation(p_hi[:, :, :], p_t[:, :, :], ACT.Copy).then_inc(phi_ready, 1)
            split_hi(N_PLE + 2)
            for g in range(4):
                leave(N_PLE, U_PLE + g, PE8[:, 2 * g:2 * g + 2, :])
            for j in range(4):
                if j < 2:
                    split_hi(N_PLEG + j + 2)
                u = U_PLEG + j
                act.wait_ge(block_used, N_PLEG + j + 1)
                if j:
                    act.wait_ge(ssq_ready, SQUARES[7] + j)
                act.activation(SG[:, :, :], halves(G[u % 4]), ACT.Sigmoid).then_inc(g_free[u % 4], 1)
            root(8)
            for q in range(4):
                src = bank_full(act, f"out{q}")
                bank_read(f"out{q}", act.activation(orow[:, q // 2, (q % 2) * 512:(q % 2) * 512 + 512],
                                                    src[:, :], ACT.Copy))


_INS = ['x', 'c', 'norm_w', 'ada_w', 'ada_b', 'attn_w_in', 'gla_w_gate', 'gla_b_gate', 'gla_norm_w',
        'attn_sinks', 'attn_w_out', 'rel_bias', 'pool_w', 'pool_scale', 'mlp_w1', 'mlp_w2', 'final_norm_w',
        'p_2', 'attn_norm_2', 'w_in_2', 'ret_norm_2', 'w_out_2', 'ffn_norm_2', 'w_up_2', 'w_gate_2',
        'conv_w_2', 'conv_b_2', 'w_down_2', 'ple_norm_2', 'w_ple_2', 'w_ple_gate_2', 'final_norm_2']
_OUTS = [((1, 256, 1024), 'float32')]


def shape_constants():
    import numpy as np

    out = np.zeros((P, C_ALL), np.float32)
    p, f = np.arange(P)[:, None], np.arange(P)[None, :]
    out[:, C_ID:C_ID + P] = p == f
    out[:, C_ANTI:C_ANTI + P] = p + f == P - 1
    dist = np.arange(P)[::-1]
    d = np.maximum(dist, 1).astype(np.float64)
    large = np.minimum(16 + (np.log(d / 16) / np.log(128 / 16) * 16).astype(np.int32), 31)
    bucket = np.where(dist < 16, dist, large)
    out[0:32, C_HOT:C_HOT + P] = np.arange(32)[:, None] == bucket[None, :]
    out[:, C_MASK:C_MASK + P] = (p // 64 == f // 64) & (p <= f)
    gap = (P + p - np.arange(S)[None, :]).astype(np.float32)
    out[:, C_DIST:C_DIST + S] = np.where(gap >= 0, -gap, np.float32(NEG))
    diff = np.arange(S)[None, :] - p
    for h in range(4):
        log_g = np.log(np.float32(1.0) - np.exp2(np.float32(-5.0 - h)), dtype=np.float32)
        decay = np.where(diff >= 0, np.exp(log_g * np.maximum(diff, 0).astype(np.float32)), 0.0)
        out[:, C_DECAY + h * S:C_DECAY + (h + 1) * S] = decay
    for g in range(4):
        out[:, C_CNT + g * POOL_PAD:C_CNT + (g + 1) * POOL_PAD] = \
            np.float32(1.0) / np.minimum(np.arange(POOL_PAD) + 1, 2 << g).astype(np.float32)
    return out


def kernel(**inputs):
    import numpy as _np
    import concourse.bacc as _bacc
    from concourse import mybir as _mybir
    from concourse.bass_utils import run_bass_kernel_spmd as _run

    nc = _bacc.Bacc("TRN2", target_bir_lowering=False, num_devices=1)
    arrays, args = {}, []
    for name in [*_INS, "shape_consts"]:
        a = _np.ascontiguousarray(inputs[name]) if name in inputs else shape_constants()
        arrays[f"in_{name}_dram"] = a
        args.append(nc.dram_tensor(f"in_{name}_dram", a.shape, _mybir.dt.from_np(a.dtype), kind="ExternalInput").ap())
    for i, (shape, dtype) in enumerate(_OUTS):
        dt = _mybir.dt.from_np(_np.dtype(dtype))
        args.append(nc.dram_tensor(f"out_{i}_dram", shape, dt, kind="ExternalOutput").ap())
    build(nc, *args)
    r = _run(nc, [arrays], core_ids=[0])
    got = tuple(r.results[0][f"out_{i}_dram"] for i in range(len(_OUTS)))
    return got[0]
```

```python
from contextlib import ExitStack

import concourse.bass as bass
from concourse import mybir

P = 128
F32 = mybir.dt.float32
F32R = mybir.dt.float32r
I32 = mybir.dt.int32
ALU = mybir.AluOpType
ACT = mybir.ActivationFunctionType
AX_X = mybir.AxisListType.X

S = 256
D = 1024
DT = D // P
COLS = 256
KT = 8
RAW = 4
FF = 4096
FF2 = 2816
F2T = FF2 // P
EPS = 1e-6
GN_EPS = 1e-5


def first_block(t):
    return ((1, 0)[t % 2], t // 2) if t < 2 * DT else (2, t - 2 * DT)

HEADS_GLA = 4
HEADS = 8
NEG = -1e30
HANKEL = 384
POOL_PAD = 16

N_ATTN, N_OUT = 0, 9
N_UP = (13, 46)
N_DOWN = (29, 62)
N_POOL = 45
N_IN2, N_OUT2, N_FFN, N_FDOWN, N_PLE, N_PLEG = 78, 92, 96, 118, 130, 131
N_ALL = 135
FDOWN_KT = (8, 8, 6)

U_POOL, U_UP, U_IN2, U_OUT2, U_FFN, U_PLE, U_PLEG = 29, (13, 33), 49, 63, 67, 89, 93

C_ID, C_ANTI, C_HOT, C_MASK, C_DIST, C_DECAY, C_CNT = 0, 128, 256, 384, 512, 768, 1792
C_ALL = C_CNT + 4 * POOL_PAD

V_NORM, V_ADAB, V_FINAL, V_ATTN2, V_FFN2, V_PLE2, V_FINAL2 = 0, 32, 128, 136, 144, 152, 160
V_RET, V_PSCALE, V_CONVB, V_GLAW, V_BGATE, V_CONVW, V_C = 168, 172, 180, 202, 203, 205, 271
V_ALL = 279

SQUARES = (4, 8, 16, None, 24, 24, 28, 36, 40)

ATT_UNITS = 8


def spread(ap, n):
    return bass.AP(ap.tensor, ap.offset, [list(ap.ap[0]), [0, n], *[list(x) for x in ap.ap[1:]]])


class Chain:

    def __init__(self, eng, sem):
        self.eng, self.sem, self.count, self.looped = eng, sem, 0, 0

    def __call__(self, ins):
        self.count += 1
        ins.then_inc(self.sem, 1)
        self.eng.wait_ge(self.sem, self.looped + self.count)


def build(nc, x, c, norm_w, ada_w, ada_b, attn_w_in, gla_w_gate, gla_b_gate, gla_norm_w, attn_sinks,
          attn_w_out, rel_bias, pool_w, pool_scale, mlp_w1, mlp_w2, final_norm_w, p_2, attn_norm_2,
          w_in_2, ret_norm_2, w_out_2, ffn_norm_2, w_up_2, w_gate_2, conv_w_2, conv_b_2, w_down_2,
          ple_norm_2, w_ple_2, w_ple_gate_2, final_norm_2, shape_consts, out):

    scratch = nc.dram_tensor("bias_rows", [HEADS, HANKEL], F32)

    def k_major(w):
        return w.rearrange("(t p) n -> p t n", p=P)

    w_in = k_major(attn_w_in[0])
    w_out1 = k_major(attn_w_out[0])
    w_up1 = [k_major(mlp_w1[n]) for n in range(2)]
    w_down1 = [k_major(mlp_w2[n]) for n in range(2)]
    w_pool = pool_w[0].rearrange("g (k p) n -> p (g k) n", p=P)
    w_in2 = k_major(w_in_2[0])
    w_out2 = k_major(w_out_2[0])
    w_up2, w_gate2 = k_major(w_up_2[0]), k_major(w_gate_2[0])
    w_down2 = k_major(w_down_2[0])
    w_ple = k_major(w_ple_2[0])
    w_pleg = k_major(w_ple_gate_2[0])
    ada = [k_major(ada_w[m // 2, m % 2]) for m in range(4)]

    ATTN_COLS = (2064, 1552, 1808, 0, 256, 512, 768, 1024, 1280)
    GLR_COL = 1536

    ctx = ExitStack()
    with ctx:
        def sb(name, shape, dt=F32, scope=ctx):
            return scope.enter_context(nc.sbuf_tensor(name, shape, dt))

        def sem(name):
            return ctx.enter_context(nc.semaphore(name))

        raw = [sb(f"raw{s}", [P, KT, COLS]) for s in range(RAW)]
        w_hi = [sb(f"w_hi{s}", [P, KT, COLS], F32R) for s in range(2)]
        w_lo = [sb(f"w_lo{s}", [P, KT, COLS], F32R) for s in range(2)]
        ada_raw = [sb(f"ada_raw{s}", [P, D]) for s in range(3)]
        ada_acc = sb("ada_acc", [P, 3, D])
        X = sb("X", [P, DT, S])
        h_hi = sb("h_hi", [P, DT, S], F32R)
        h_lo = sb("h_lo", [P, DT, S], F32R)
        HN = [sb(f"HN{s}", [P, 2, S]) for s in range(2)]
        sq_sum = sb("sq_sum", [P, 2, S])
        sq = sb("sq", [P, 2, S])
        ln_ms = sb("ln_ms", [P, S])
        rstd = sb("rstd", [P, S])
        unused = sb("unused", [P, 1])
        ones = sb("ones", [P, P])
        eps6 = sb("eps6", [P, 1])
        eps5 = sb("eps5", [P, 1])
        one = sb("one", [P, 1])
        C = sb("C", [P, C_DECAY + 4 * POOL_PAD])
        V = sb("V", [P, V_ALL])
        c_silu = sb("c_silu", [P, DT])
        c_tmp = sb("c_tmp", [P, DT])
        MOD = sb("MOD", [P, 4, 3 * DT])
        GAIN = sb("GAIN", [P, 4, DT])
        gate_ps = sb("gate_ps", [P, DT])
        final_sq = sb("final_sq", [P, DT])
        t_ln, t_rstd = sb("t_ln", [P, 2]), sb("t_rstd", [P, 2])

        with ExitStack() as att:
            MIX = sb("MIX", [P, DT, S], F32, att)
            BIAS = sb("BIAS", [P, HEADS, S], F32, att)
            Q4 = sb("Q4", [P, 4, S], F32, att)
            K4 = sb("K4", [P, 4, S], F32, att)
            V4 = sb("V4", [P, 2, 512], F32, att)
            SS = sb("SS", [P, 2, 2, S], F32, att)
            PR = sb("PR", [P, 2, 2, S], F32, att)
            PT = sb("PT", [P, 2, 4, P], F32, att)
            stat = sb("stat", [P, 2, 8], F32, att)
            sinks = sb("sinks", [P, HEADS], F32, att)
            wide = sb("wide", [P, 8, 512], F32, att)
            GV = sb("GV", [P, 2, 512], F32, att)
            GG = sb("GG", [P, 4, S], F32, att)
            GE = sb("GE", [P, 4, S], F32, att)
            reset = sb("reset", [P, 2 * S], F32, att)
            ST = sb("ST", [P, HEADS_GLA, 3, P], F32, att)
            g_hi = sb("g_hi", [P, DT, 16], F32R, att)
            g_lo = sb("g_lo", [P, DT, 16], F32R, att)
            g_raw = sb("g_raw", [P, DT, 16], F32, att)
            w_gla = sb("w_gla", [16, S], F32, att)
            GLT = sb("GLT", [P, 2, 16], F32, att)
            GL = sb("GL", [16, S], F32, att)
            rb = sb("rb", [32, HEADS], F32, att)
        with ExitStack() as mlp:
            u_hi = sb("u_hi", [P, FF // P, S], F32R, mlp)
            u_lo = sb("u_lo", [P, FF // P, S], F32R, mlp)
            late_acc = sb("late_acc", [P, 3, D], F32, mlp)
        with ExitStack() as pooling:
            pad = [sb(f"pad{s}", [P, DT, POOL_PAD + S], F32, pooling) for s in range(2)]
            win = sb("win", [P, DT, POOL_PAD + S], F32, pooling)
        with ExitStack() as gated:
            f_hi = sb("f_hi", [P, F2T, S], F32R, gated)
            f_lo = sb("f_lo", [P, F2T, S], F32R, gated)
            UP = sb("UP", [P, 2, 2 + S], F32, gated)
            CV = sb("CV", [P, 2, S], F32, gated)
            GU = sb("GU", [P, 2, S], F32, gated)
            PE8 = sb("PE8", [P, DT, S], F32, gated)
            SG = sb("SG", [P, 2, S], F32, gated)
            p_hi = sb("p_hi", [P, 2, S], F32R, gated)
            p_lo = sb("p_lo", [P, 2, S], F32R, gated)
            p_rows = sb("p_rows", [P, 2, S], F32, gated)
            p_t = SG
            orow = sb("orow", [P, 2, D], F32, gated)

        relu = HN
        pool_squares = (sq_sum, sq, *HN)
        ln_ms5, rstd5 = sq[:, 0, :], sq[:, 1, :]
        early = [raw[1 + n // 2][:, 4 * (n % 2):4 * (n % 2) + 4, :].rearrange("p k n -> p (k n)")
                 for n in range(6)]
        sums_of = (ada_acc, ada_acc, ada_acc, late_acc)

        GQ, GK, GZ, GA, GB, EB, ENB, KE = (
            wide[:, n, :].rearrange("p (t s) -> p t s", t=2) for n in range(8))
        RQ, RK, RG, RT = (
            wide[:, 2 * n:2 * n + 2, :].rearrange("p a b -> p (a b)").rearrange("p (t s) -> p t s", t=4)
            for n in range(4))
        x_rows = wide[:, 0:4, :].rearrange("p (k a) b -> p k (a b)", k=2)
        hankel = MIX
        t8 = SS[0:HEADS, :, :, :].rearrange("p a b s -> p (a b s)")[:, 0:HANKEL]
        vrows = PR[:, 0, :, :].rearrange("p a s -> p (a s)").rearrange("p (n s) -> p n s", n=4)
        ident, anti = C[:, C_ID:C_ID + P], C[:, C_ANTI:C_ANTI + P]
        chunk_mask = C[:, C_MASK:C_MASK + P].bitcast(I32)
        C_CNT_AT = C_DECAY
        KET = wide[:, 3, :].rearrange("p (a s) -> p a s", a=4)
        AM = wide[:, 6:8, :].rearrange("p k (h s) -> p k h s", h=4)
        O = PR[:, :, :, :].rearrange("p a b s -> p (a b) s")
        OSQ, RO = BIAS[:, 0:4, :], BIAS[:, 4:8, :]
        RS = [b[:, :, :, :].rearrange("p a b s -> p (a b s)")[:, k * 384:(k + 1) * 384]
              for b in (SS, PR) for k in range(2)]
        V4r = GE[:, :, :].rearrange("p t s -> p (t s)").rearrange("p (k f) -> p k f", k=2)
        DECAY = GV[:, :, :].rearrange("p a (b c) -> p (a b) c", c=S)

        G = [ctx.enter_context(nc.psum_tensor(f"G{n}", [P, 512], F32)) for n in range(4)]
        A = [ctx.enter_context(nc.psum_tensor(f"A{n}", [P, 512], F32)) for n in range(4)]

        def halves(bank):
            return bank[:, :].rearrange("p (t s) -> p t s", t=2)

        def sems(*names):
            return [sem(n) for n in names]

        consts_in, vecs_in, x_in, small_in, glr_in, table_out, table_in, decay_in, p_in, out_done = sems(
            "consts_in", "vecs_in", "x_in", "small_in", "glr_in", "table_out", "table_in", "decay_in",
            "p_in", "out_done")
        raw_full = sems(*(f"raw_full{n}" for n in range(RAW)))
        ada_full = sems(*(f"ada_full{n}" for n in range(3)))
        early_full = sems(*(f"early_full{n}" for n in range(6)))
        hi_done, lo_done, block_used, ada_used = sems("hi_done", "lo_done", "block_used", "ada_used")
        g_free = sems(*(f"g_free{n}" for n in range(4)))
        a_full = sems(*(f"a_full{n}" for n in range(4)))
        a_free = sems(*(f"a_free{n}" for n in range(4)))
        down_half, down_free0, down_free1 = sems("down_half", "down_free0", "down_free1")
        dve_step, act_step, pe_step = sems("dve_step", "act_step", "pe_step")
        norm_ready, hhi_ready, h_ready, ssq_ready, rstd_ready, ms5_scaled = sems(
            "norm_ready", "hhi_ready", "h_ready", "ssq_ready", "rstd_ready", "ms5_scaled")
        acc_clear, mod_ready, setup_ready, c_sigmoid = sems("acc_clear", "mod_ready", "setup_ready", "c_sigmoid")
        g_split, g_ready, max_ready, prob_ready, prob_scaled, mix_ready = sems(
            "g_split", "g_ready", "max_ready", "prob_ready", "prob_scaled", "mix_ready")
        z_ready, decay_ready, exp_ready, gla_ready, osq_ready, ors_ready = sems(
            "z_ready", "decay_ready", "exp_ready", "gla_ready", "osq_ready", "ors_ready")
        uhi_ready, u_ready, pool_normed, pool_shifted, pool_squared = sems(
            "uhi_ready", "u_ready", "pool_normed", "pool_shifted", "pool_squared")
        pads_ready, conv_ready, gelu_ready, fhi_ready, f_ready = sems(
            "pads_ready", "conv_ready", "gelu_ready", "fhi_ready", "f_ready")
        phi_ready, p_ready, fin_ready, token_ms, token_rstd, rows_dve, rows_act = sems(
            "phi_ready", "p_ready", "fin_ready", "token_ms", "token_rstd", "rows_dve", "rows_act")

        USE, uses = {}, [0] * 4

        def take(name, bank):
            USE[name] = (bank, uses[bank])
            uses[bank] += 1

        def take_attention(r, v):
            if v < ATT_UNITS:
                take(f"scores{r}{v}", v % 2)
            if 1 <= v <= ATT_UNITS:
                take(f"turned{r}{v - 1}", 2)
            if v >= 2:
                take(f"att_out{r}{v - 2}", 3)

        def take_each(*names):
            for name, bank in names:
                take(name, bank)

        take_each(("vecs", 0), ("table", 1), ("x0", 2), ("x1", 3), ("x2", 0), ("x3", 1), ("flip0", 2),
                  ("flip1", 3), ("flip2", 0), ("flip3", 1), ("ms0", 2), ("mod0", 3), ("glr", 2))
        take_attention(0, 0)
        take("glt", 3)
        take_attention(0, 1)
        take("logits", 3)
        take_attention(0, 2)
        take("gate0", 3)
        for v in range(3, 6):
            take_attention(0, v)
        take("kend", 2)
        take_attention(0, 6)
        take_each(("gs0", 0), ("gs1", 1))
        take_attention(0, 7)
        take_each(("ds0", 2), ("ds1", 3))
        take_attention(0, 8)
        take("ds2", 2)
        take_attention(0, 9)
        take_each(("go0", 0), ("go1", 1), ("gm0", 2), ("gm1", 3), ("mod1", 3), ("ms1", 2), ("gate1", 3),
                  ("mod2", 3), ("ms2", 2), ("gate2", 0), ("mod3", 1), ("gate3", 3), ("ms3", 2), ("ms4", 2), ("ms5", 3))
        for v in range(ATT_UNITS + 2):
            take_attention(1, v)
        take_each(*((f"rs{h}", h % 2) for h in range(4)))
        take_each(("ro0", 2), ("ro1", 3), ("rm0", 0), ("rm1", 1), ("rv0", 2), ("rv1", 3), ("ms6", 2),
                  ("ms7", 2), ("pt", 3), ("out0", 0), ("out1", 1), ("out2", 2), ("out3", 3))

        def bank_empty(pe, name):
            bank, before = USE[name]
            if before:
                pe.wait_ge(a_free[bank], before)
            return A[bank]

        def bank_done(name, ins):
            ins.then_inc(a_full[USE[name][0]], 1)

        def bank_full(eng, name):
            bank, before = USE[name]
            eng.wait_ge(a_full[bank], before + 1)
            return A[bank]

        def bank_read(name, ins):
            ins.then_inc(a_free[USE[name][0]], 1)

        def bank_was_read(eng, name):
            bank, before = USE[name]
            eng.wait_ge(a_free[bank], before + 1)

        SPLIT = {"n0": 0, "mix0": 1, "n1": 2, "pool": 3, "n3": 4, "n5": 5, "mix1": 6, "n6": 7, "n7": 8}
        NORMED = {"n0": 0, "n1": 1, "pool": 2, "n3": 3, "n5": 4, "n6": 5, "n7": 6}

        def k_tiles(n):
            return FDOWN_KT[(n - N_FDOWN) % 3] if N_FDOWN <= n < N_PLE else KT

        block = ctx.enter_context(nc.Block())

        @block.sync
        def _(sp):
            def load(n, src, i=0):
                if n >= RAW:
                    sp.wait_ge(lo_done, n - RAW + 1 + i * 4)
                sp.dma_start(raw[n % RAW][:, 0:k_tiles(n), :], src).then_inc(raw_full[n % RAW], 16)

            with nc.allow_non_contiguous_dma(reason="weight blocks"):
                sp.dma_start(C[:, 0:C_DECAY], shape_consts[:, 0:C_DECAY]).then_inc(consts_in, 16)
                sp.dma_start(C[:, C_DECAY:], shape_consts[:, C_CNT:C_ALL]).then_inc(consts_in, 16)
                rows = [(norm_w.rearrange("l s (t p) -> (l s t) p", p=P), 32, 0, 0),
                        (ada_b.rearrange("l s (t p) -> (l s t) p", p=P), 96, 0, 32)]
                at = 0
                for vec in (final_norm_w, attn_norm_2, ffn_norm_2, ple_norm_2, final_norm_2, ret_norm_2,
                            pool_scale, conv_b_2, gla_norm_w, gla_b_gate):
                    flat = vec if len(vec.shape) == 1 else vec.rearrange("a d -> (a d)")
                    r = flat.rearrange("(t p) -> t p", p=P)
                    rows.append((r, r.shape[0], 1, at))
                    at += r.shape[0]
                rows.append((conv_w_2[0].rearrange("j (t p) -> (j t) p", p=P), 3 * F2T, 2, 0))
                rows.append((c[0].rearrange("(t p) -> t p", p=P), DT, 3, 0))
                for r, count, slot, at in rows:
                    sp.dma_start(vrows[at:at + count, slot, :], r).then_inc(vecs_in, 16)
                sp.dma_start(x_rows, x[0].rearrange("(k p) d -> p k d", p=P)).then_inc(x_in, 16)
                sp.dma_start(rb[:, :], rel_bias).then_inc(small_in, 16)
                sp.dma_start(w_gla[:, :], gla_w_gate[0]).then_inc(small_in, 16)
                sp.dma_start(sinks[:, :], bass.AP(attn_sinks.tensor, attn_sinks.offset, [[0, P], [1, HEADS]])
                             ).then_inc(small_in, 16)
                sp.dma_start(g_raw[:, :, :], w_in[:, :, GLR_COL:GLR_COL + 16]).then_inc(glr_in, 16)
                bank_was_read(sp, "table")
                sp.dma_start(scratch.ap(), t8[:, :]).then_inc(table_out, 16)
                sp.wait_ge(table_out, 16)
                sp.dma_start(hankel[:, :, :],
                             bass.AP(scratch, 0, [[1, P], [HANKEL, HEADS], [1, S]])).then_inc(table_in, 16)
                for j, col in enumerate(ATTN_COLS):
                    if 1 <= j < RAW:
                        sp.wait_ge(ada_used, (14, 16, 17)[j - 1])
                    load(N_ATTN + j, w_in[:, :, col:col + COLS])
                for j in range(4):
                    load(N_OUT + j, w_out1[:, :, j * COLS:(j + 1) * COLS])
                for layer in range(2):
                    with sp.Fori(0, 4) as i:
                        for j in range(4):
                            load(N_UP[layer] + j, w_up1[layer][:, :, bass.ds(i * 4 * COLS + j * COLS, COLS)], i)
                    with sp.Fori(0, 4) as i:
                        for j in range(4):
                            load(N_DOWN[layer] + j,
                                 w_down1[layer][:, j * KT:(j + 1) * KT, bass.ds(i * COLS, COLS)], i)
                    if layer == 0:
                        load(N_POOL, w_pool)
                for j in range(14):
                    load(N_IN2 + j, w_in2[:, :, j * COLS:(j + 1) * COLS])
                    if j == 4:
                        sp.wait_ge(h_ready, 4 * SPLIT["n5"] + 1)
                        sp.dma_start(DECAY, shape_consts[:, C_DECAY:C_CNT].rearrange(
                            "p (h s) -> p h s", h=4)).then_inc(decay_in, 16)
                for j in range(4):
                    load(N_OUT2 + j, w_out2[:, :, j * COLS:(j + 1) * COLS])
                with sp.Fori(0, 5) as i:
                    for j in range(4):
                        w = w_up2 if j % 2 == 0 else w_gate2
                        load(N_FFN + j, w[:, :, bass.ds(i * 2 * COLS + (j // 2) * COLS, COLS)], i)
                for j in (20, 21):
                    w = w_up2 if j % 2 == 0 else w_gate2
                    load(N_FFN + j, w[:, :, 10 * COLS:11 * COLS])
                sp.wait_ge(h_ready, 4 * SPLIT["n6"] + 1)
                sp.dma_start(p_rows[:, :, :], p_2[0, 0].rearrange("(k p) d -> p k d", p=P)).then_inc(p_in, 16)
                for g in range(4):
                    for j in range(3):
                        load(N_FDOWN + 3 * g + j,
                             w_down2[:, j * KT:j * KT + FDOWN_KT[j], g * COLS:(g + 1) * COLS])
                sp.wait_ge(lo_done, N_PLE - RAW + 1)
                sp.dma_start(raw[N_PLE % RAW][:, :, :].rearrange("p (k g) n -> p k (g n)", k=2), w_ple
                             ).then_inc(raw_full[N_PLE % RAW], 16)
                for j in range(4):
                    load(N_PLEG + j, w_pleg[:, :, j * COLS:(j + 1) * COLS])
                for k in range(2):
                    sp.wait_ge(rows_dve, k + 1)
                    sp.wait_ge(rows_act, k + 1)
                    sp.dma_start(out[0, k * P:(k + 1) * P, :], orow[:, k, :]).then_inc(out_done, 16)
                sp.wait_ge(out_done, 32)

        @block.gpsimd
        def _(pool):
            def load(m, slot, k, part):
                pool.dma_start(ada_raw[slot][:, :], ada[m][:, k, part * D:(part + 1) * D]).then_inc(
                    ada_full[slot], 16)

            for t in range(3 * DT):
                part, k = first_block(t)
                if t == 3:
                    pool.wait_ge(vecs_in, 16 * 14)
                if 3 <= t < 9:
                    pool.dma_start(early[t - 3], ada[0][:, k, part * D:(part + 1) * D]).then_inc(
                        early_full[t - 3], 16)
                    continue
                if t >= 9:
                    pool.wait_ge(ada_used, t - 8 if t < 12 else t - 2)
                load(0, t % 3, k, part)
            def load_at(m, part, i):
                pool.dma_start(ada_raw[part][:, :],
                               ada[m][:, bass.ds(i, 1), part * D:(part + 1) * D].rearrange(
                                   "p a n -> p (a n)")).then_inc(ada_full[part], 16)

            for m in (1, 2):
                for part in range(3):
                    pool.wait_ge(ada_used, 3 * DT * m + part - 2)
                    load(m, part, 0, part)
                if m == 2:
                    bank_full(pool, "gate1")
                    pool.memset(ada_acc[:, :, :], 0.0)
                    pool.memset(late_acc[:, :, :], 0.0).then_inc(acc_clear, 1)
                with pool.Fori(1, DT) as i:
                    for part in range(3):
                        pool.wait_ge(ada_used, i * 3 + (3 * DT * m + part - 2))
                        load_at(m, part, i)
            with pool.Fori(0, DT) as i:
                for part in range(2):
                    pool.wait_ge(ada_used, i * 2 + (9 * DT + part - 1))
                    load_at(3, part, i)
            with pool.Fori(0, DT) as i:
                pool.wait_ge(ada_used, i + 11 * DT)
                load_at(3, 2, i)

        @block.tensor
        def _(pe):
            chain = Chain(pe, pe_step)

            def product(dst, wh, wl, ah, al, start, stop):
                pe.matmul(dst, wh, ah, start=start, stop=False)
                pe.matmul(dst, wh, al, start=False, stop=False)
                return pe.matmul(dst, wl, ah, start=False, stop=stop)

            def block_ready(n, i=0):
                pe.wait_ge(lo_done, n + 1 + i * 4)

            def g_empty(u, i=0):
                if u >= 4:
                    pe.wait_ge(g_free[u % 4], u // 4 + i)

            def feature_tile(n, dst, cols, kts, hi, lo, start=True, stop=True, split=None):
                for a, (kb, ka) in enumerate(kts):
                    if split and a % 2 == 0:
                        pe.wait_ge(h_ready, 4 * SPLIT[split] + a // 2 + 1)
                    last = product(dst, w_hi[n % 2][:, kb, cols], w_lo[n % 2][:, kb, cols],
                                   hi[:, ka, :], lo[:, ka, :], start and a == 0, stop and a == len(kts) - 1)
                return last

            def feature_block(n, u, split=None, i=0, order=range(KT)):
                block_ready(n, i)
                g_empty(u, i)
                for m in range(2):
                    last = feature_tile(n, halves(G[u % 4])[:, m, :], slice(m * P, m * P + P),
                                        [(k, k) for k in order], h_hi, h_lo, split=split if m == 0 else None)
                last.then_inc(block_used, 1)

            def token_tile(n, dst, k, cols):
                for t in range(KT):
                    toks = slice(k * P, k * P + P)
                    pe.matmul(dst, h_hi[:, t, toks], w_hi[n % 2][:, t, cols], start=t == 0, stop=False)
                    pe.matmul(dst, h_hi[:, t, toks], w_lo[n % 2][:, t, cols], start=False, stop=False)
                    last = pe.matmul(dst, h_lo[:, t, toks], w_hi[n % 2][:, t, cols], start=False,
                                     stop=t == KT - 1)
                return last

            def token_block(n, u):
                block_ready(n)
                g_empty(u)
                for k in range(2):
                    last = token_tile(n, halves(G[u % 4])[:, k, :], k, slice(0, COLS))
                last.then_inc(block_used, 1)

            def mean_square(norm, squares=sq_sum):
                pe.wait_ge(ssq_ready, SQUARES[norm])
                dst = bank_empty(pe, f"ms{norm}")
                for m in range(2):
                    last = pe.matmul(dst[:, 0:S], ones[:, :], squares[:, m, :], start=m == 0, stop=m == 1)
                bank_done(f"ms{norm}", last)

            def modulation(name, m, parts):
                dst = bank_empty(pe, name)
                for part, blocks in parts:
                    pe.wait_ge(ada_used, blocks)
                    for t in range(DT):
                        last = pe.matmul(dst[:, part * DT + t:part * DT + t + 1],
                                         sums_of[m][:, part, t * P:(t + 1) * P], ones[:, 0:1],
                                         start=True, stop=True)
                bank_done(name, last)

            def scale_and_shift(m):
                modulation(f"mod{m}", m, [(part, 11 * DT if m == 3 else 3 * DT * (m + 1)) for part in (1, 0)])

            def gate_sums(m):
                modulation(f"gate{m}", m, [(2, 3 * DT * (m + 1))])

            def attention(r, v):
                if v < ATT_UNITS:
                    hp, b = v // 2, v % 2
                    dst = halves(bank_empty(pe, f"scores{r}{v}"))
                    keys = S if b else P
                    for e in range(2):
                        kt = hp if r else int(hp // 2 != e)
                        half = slice(64 * e, 64 * e + 64)
                        last = pe.matmul(dst[:, e, 0:keys], Q4[half, hp, b * P:b * P + P],
                                         K4[half, kt, 0:keys], start=True, stop=True)
                        if e == 0:
                            chain(last)
                    bank_done(f"scores{r}{v}", last)
                if 1 <= v <= ATT_UNITS:
                    w = v - 1
                    pe.wait_ge(prob_scaled, ATT_UNITS * r + w + 1)
                    dst = bank_empty(pe, f"turned{r}{w}")
                    for e in range(2):
                        for k in range(w % 2 + 1):
                            at = (2 * e + k) * P
                            last = pe.transpose(dst[:, at:at + P], PR[:, w % 2, e, k * P:k * P + P], ident)
                    bank_done(f"turned{r}{w}", last)
                if v >= 2:
                    w = v - 2
                    hp, b = w // 2, w % 2
                    bank_was_read(pe, f"turned{r}{w}")
                    dst = bank_empty(pe, f"att_out{r}{w}")
                    for e in range(2):
                        col = (2 * hp + e) * 64 if r else hp // 2 * 64
                        for k in range(b + 1):
                            last = pe.matmul(dst[64 * e:64 * e + 64, 0:P], V4[:, k, col:col + 64],
                                             PT[:, w % 2, 2 * e + k, :], start=k == 0, stop=k == b)
                    bank_done(f"att_out{r}{w}", last)

            pe.wait_ge(consts_in, 32)
            pe.wait_ge(vecs_in, 16 * 14)
            dst = bank_empty(pe, "vecs")
            for slot, count, at in ((0, P, 0), (1, 77, 128), (2, 3 * F2T, V_CONVW), (3, DT, V_C)):
                last = pe.transpose(dst[:, at:at + count], vrows[0:count, slot, :],
                                    C[0:count, C_ID:C_ID + count])
            bank_done("vecs", last)
            pe.wait_ge(small_in, 48)
            bank_done("table", pe.matmul(bank_empty(pe, "table")[0:HEADS, 0:P], rb[:, :],
                                         C[0:32, C_HOT:C_HOT + P], start=True, stop=True))
            pe.wait_ge(x_in, 16)
            for q in range(4):
                dst = bank_empty(pe, f"x{q}")
                for t in range(2):
                    for k in range(2):
                        last = pe.transpose(dst[:, t * S + k * P:t * S + k * P + P],
                                            x_rows[:, k, (2 * q + t) * P:(2 * q + t + 1) * P], ident)
                bank_done(f"x{q}", last)
            pe.wait_ge(table_in, 16)
            for q in range(4):
                dst = bank_empty(pe, f"flip{q}")
                bank_done(f"flip{q}", pe.matmul(halves(dst), anti, hankel[:, 2 * q:2 * q + 2, :],
                                                start=True, stop=True))
            mean_square(0)
            modulation("mod0", 0, [(1, 2 * DT - 1), (0, 2 * DT)])

            block_ready(0)
            last = feature_tile(0, G[0][:, 0:S], slice(0, P), [(k, k) for k in range(KT)], h_hi, h_lo,
                                split="n0")
            for k in range(2):
                last = token_tile(0, G[0][:, S + k * P:S + (k + 1) * P], k, slice(P, 2 * P))
            last.then_inc(block_used, 1)
            feature_block(1, 1)
            pe.wait_ge(g_ready, 1)
            dst = bank_empty(pe, "glr")
            for k in range(2):
                for t in range(DT):
                    toks = slice(k * P, k * P + P)
                    o = dst[:, k * 16:k * 16 + 16]
                    pe.matmul(o, h_hi[:, t, toks], g_hi[:, t, :], start=t == 0, stop=False)
                    pe.matmul(o, h_hi[:, t, toks], g_lo[:, t, :], start=False, stop=False)
                    last = pe.matmul(o, h_lo[:, t, toks], g_hi[:, t, :], start=False, stop=t == DT - 1)
            bank_done("glr", last)
            pe.wait_ge(g_free[0], 1)
            pe.wait_ge(g_free[1], 1)
            attention(0, 0)
            feature_block(2, 2)
            bank_was_read(pe, "glr")
            dst = bank_empty(pe, "glt")
            for k in range(2):
                last = pe.transpose(dst[0:16, k * P:k * P + P], GLT[:, k, :], ident)
            bank_done("glt", last)
            attention(0, 1)
            feature_block(3, 3)
            bank_was_read(pe, "glt")
            dst = bank_empty(pe, "logits")
            for m in range(2):
                last = pe.matmul(dst[:, m * S:m * S + S], w_gla[:, m * P:m * P + P], GL[:, :],
                                 start=True, stop=True)
            bank_done("logits", last)
            attention(0, 2)
            feature_block(4, 4)
            gate_sums(0)
            attention(0, 3)
            token_block(5, 5)
            pe.wait_ge(g_free[2], 1)
            attention(0, 4)
            token_block(6, 6)
            attention(0, 5)
            feature_block(7, 7)
            pe.wait_ge(gla_ready, 1)
            dst = bank_empty(pe, "kend")
            for m in range(2):
                for k in range(2):
                    at = (2 * m + k) * P
                    last = pe.transpose(dst[:, at:at + P], KE[:, m, k * P:k * P + P], ident)
            bank_done("kend", last)
            attention(0, 6)
            for k in range(2):
                dst = bank_empty(pe, f"gs{k}")
                for h in (0, 2, 1, 3):
                    half = slice(64 * (h % 2), 64 * (h % 2) + 64)
                    last = pe.matmul(dst[:, h * P:h * P + P], GK[half, h // 2, k * P:k * P + P],
                                     GQ[half, h // 2, k * P:k * P + P], start=True, stop=True)
                    if h == 2:
                        chain(last)
                bank_done(f"gs{k}", last)
            feature_block(8, 8)
            attention(0, 7)
            bank_was_read(pe, "kend")
            pe.wait_ge(g_free[1], 2)
            pe.wait_ge(g_free[2], 2)

            def increments(name, steps):
                dst = bank_empty(pe, name)
                for a, (m, ch) in enumerate(steps):
                    rows = slice(64 * (ch % 2), 64 * (ch % 2) + 64)
                    last = pe.matmul(dst[:, a * S:a * S + S], KET[rows, 2 * m + ch // 2, :],
                                     GV[rows, ch // 2, m * S:m * S + S], start=True, stop=True)
                    if a == 0 and name != "ds2":
                        chain(last)
                bank_done(name, last)

            increments("ds0", ((0, 0), (0, 1)))
            increments("ds1", ((1, 0), (1, 1)))
            attention(0, 8)
            increments("ds2", ((0, 2), (1, 2)))
            attention(0, 9)
            for name in ("gs0", "gs1", "ds2"):
                bank_was_read(pe, name)
            for m in range(2):
                dst = bank_empty(pe, f"go{m}")
                for e in range(2):
                    h = 2 * m + e
                    for k in range(2):
                        at = e * S + k * P
                        last = pe.matmul(dst[:, at:at + P], GV[:, k, h * P:h * P + P], AM[:, k, h, :],
                                         start=True, stop=False, skip_group_check=True)
                        for ch in range(max(2 * k, 1), 2 * k + 2):
                            at = e * S + ch * 64
                            last = pe.matmul(dst[:, at:at + 64], ST[:, h, ch - 1, :],
                                             GQ[:, m, ch * 64:ch * 64 + 64], start=False,
                                             stop=ch % 2 == 1, skip_group_check=True)
                bank_done(f"go{m}", last)
            for m in range(2):
                pe.wait_ge(osq_ready, m + 1)
                dst = bank_empty(pe, f"gm{m}")
                bank_done(f"gm{m}", pe.matmul(halves(dst), ones[:, :], OSQ[:, 2 * m:2 * m + 2, :],
                                              start=True, stop=True))
            for j in range(4):
                feature_block(N_OUT + j, 9 + j, split="mix0" if j == 0 else None,
                              order=(4, 5, 6, 7, 0, 1, 2, 3))

            def up(layer):
                with pe.Fori(0, 4) as i:
                    for j in range(4):
                        feature_block(N_UP[layer] + j, U_UP[layer] + j, i=i,
                                      split=("n1", "n3")[layer] if j == 0 else None)

            def down(layer):
                with pe.Fori(0, 4) as i:
                    for j in range(4):
                        n = N_DOWN[layer] + j
                        block_ready(n, i)
                        pe.wait_ge(u_ready, 16 * layer + 4 * j + 4)
                        for m in range(2):
                            if j == 0:
                                pe.wait_ge((down_free0, down_free1)[m], i + (5 * layer + 1))
                            last = feature_tile(n, A[m][:, 0:S], slice(m * P, m * P + P),
                                                [(k, KT * j + k) for k in range(KT)], u_hi, u_lo,
                                                start=j == 0, stop=j == 3)
                            if m == 0 and j == 3:
                                last.then_inc(down_half, 1)
                        last.then_inc(block_used, 1)

            scale_and_shift(1)
            mean_square(1)
            gate_sums(1)
            up(0)
            down(0)
            scale_and_shift(2)
            mean_square(2)
            gate_sums(2)
            scale_and_shift(3)
            block_ready(N_POOL)
            for g in range(4):
                g_empty(U_POOL + g)
                for m in range(2):
                    if m == 0:
                        pe.wait_ge(h_ready, 4 * SPLIT["pool"] + g + 1)
                    last = feature_tile(N_POOL, halves(G[(U_POOL + g) % 4])[:, m, :], slice(m * P, m * P + P),
                                        [(2 * g, 2 * g), (2 * g + 1, 2 * g + 1)], h_hi, h_lo)
            last.then_inc(block_used, 1)
            dst = bank_empty(pe, "ms3")
            for g in range(4):
                pe.wait_ge(pool_squared, g + 1)
                for m in range(2):
                    last = pe.matmul(dst[:, 0:S], ones[:, :], pool_squares[g][:, m, :],
                                     start=g == 0 and m == 0, stop=g == 3 and m == 1)
            bank_done("ms3", last)
            up(1)
            gate_sums(3)
            down(1)
            mean_square(4)
            mean_square(5, HN[1])

            feature_block(N_IN2, U_IN2, split="n5")
            feature_block(N_IN2 + 1, U_IN2 + 1)
            feature_block(N_IN2 + 2, U_IN2 + 2)

            def retention_scores(heads):
                for h in heads:
                    dst = bank_empty(pe, f"rs{h}")
                    pe.matmul(dst[:, 0:S], RK[:, h, 0:P], RQ[:, h, :], start=True, stop=True)
                    last = pe.matmul(dst[:, S:S + P], RK[:, h, P:S], RQ[:, h, P:S], start=True, stop=True)
                    bank_done(f"rs{h}", last)

            for j in range(3, 14):
                if j in (4, 5, 10, 11):
                    token_block(N_IN2 + j, U_IN2 + j)
                else:
                    feature_block(N_IN2 + j, U_IN2 + j)
                for v, blocks in ((0, (0, 2)), (2, (4,)), (4, (1, 3)), (6, (5,))):
                    if j - 3 == v:
                        for u in (U_IN2 + n for n in blocks):
                            pe.wait_ge(g_free[u % 4], u // 4 + 1)
                if j < 13:
                    attention(1, j - 3)
                if j == 12:
                    for u in range(U_IN2 + 8, U_IN2 + 12):
                        pe.wait_ge(g_free[u % 4], u // 4 + 1)
                    retention_scores((0, 1))
            retention_scores((2, 3))
            for h in range(4):
                m, e = h // 2, h % 2
                bank_was_read(pe, f"rs{h}")
                if e == 0:
                    dst = bank_empty(pe, f"ro{m}")
                pe.matmul(dst[:, e * S:e * S + S], V4r[:, 0, h * P:h * P + P], RS[h][:, 0:S],
                          start=True, stop=False, skip_group_check=True)
                last = pe.matmul(dst[:, e * S + P:e * S + S], V4r[:, 1, h * P:h * P + P], RS[h][:, S:S + P],
                                 start=False, stop=True, skip_group_check=True)
                if e == 1:
                    bank_done(f"ro{m}", last)
            for name, src in (("rm", GG), ("rv", OSQ)):
                for m in range(2):
                    if name == "rm":
                        bank_was_read(pe, f"ro{m}")
                    else:
                        pe.wait_ge(osq_ready, 2 + m + 1)
                    dst = bank_empty(pe, f"{name}{m}")
                    bank_done(f"{name}{m}", pe.matmul(halves(dst), ones[:, :], src[:, 2 * m:2 * m + 2, :],
                                                      start=True, stop=True))
            for j in range(4):
                feature_block(N_OUT2 + j, U_OUT2 + j, split="mix1" if j == 0 else None)
            mean_square(6)
            with pe.Fori(0, 5) as i:
                for j in range(4):
                    feature_block(N_FFN + j, U_FFN + j, i=i, split="n6" if j == 0 else None)
            for j in (20, 21):
                feature_block(N_FFN + j, U_FFN + j)
            for g in range(4):
                for j in range(3):
                    n = N_FDOWN + 3 * g + j
                    block_ready(n)
                    pe.wait_ge(f_ready, (4, 8, 11)[j])
                    for m in range(2):
                        if j == 0:
                            pe.wait_ge((down_free0, down_free1)[m], 11 + g)
                        last = feature_tile(n, A[m][:, 0:S], slice(m * P, m * P + P),
                                            [(k, KT * j + k) for k in range(FDOWN_KT[j])], f_hi, f_lo,
                                            start=j == 0, stop=j == 2)
                        if m == 0 and j == 2:
                            last.then_inc(down_half, 1)
                    last.then_inc(block_used, 1)
                if g == 0:
                    pe.wait_ge(p_in, 16)
                    dst = bank_empty(pe, "pt")
                    for t in range(2):
                        for k in range(2):
                            last = pe.transpose(dst[:, t * S + k * P:t * S + k * P + P],
                                                p_rows[:, k, t * P:t * P + P], ident)
                    bank_done("pt", last)
            pe.wait_ge(p_ready, 1)
            block_ready(N_PLE)
            for g in range(4):
                g_empty(U_PLE + g)
                for m in range(2):
                    last = feature_tile(N_PLE, halves(G[(U_PLE + g) % 4])[:, m, :], slice(m * P, m * P + P),
                                        [(g, 0), (4 + g, 1)], p_hi, p_lo)
                if g == 0:
                    mean_square(7)
            last.then_inc(block_used, 1)
            def turn_out(q):
                pe.wait_ge(fin_ready, q + 1)
                dst = bank_empty(pe, f"out{q}")
                for k in range(2):
                    for t in range(2):
                        at = (2 * k + t) * P
                        last = pe.transpose(dst[:, at:at + P], X[:, 2 * q + t, k * P:k * P + P], ident)
                bank_done(f"out{q}", last)

            for j in range(4):
                feature_block(N_PLEG + j, U_PLEG + j, split="n7" if j == 0 else None)
                if j == 2:
                    turn_out(0)
            turn_out(1)
            turn_out(2)
            u = U_PLEG + 4
            pe.wait_ge(ssq_ready, SQUARES[8])
            g_empty(u)
            for k in range(2):
                for m in range(2):
                    last = pe.matmul(G[u % 4][:, k:k + 1], sq_sum[:, m, k * P:k * P + P], ones[:, 0:1],
                                     start=m == 0, stop=m == 1)
            last.then_inc(token_ms, 1)
            turn_out(3)

        @block.vector
        def _(dve):
            chain = Chain(dve, dve_step)
            ada_at = [0]

            def split_lo(n, i=0):
                k = k_tiles(n)
                dve.wait_ge(hi_done, n + 1 + i * 4)
                dve.tensor_tensor(w_lo[n % 2][:, 0:k, :], raw[n % RAW][:, 0:k, :],
                                  w_hi[n % 2][:, 0:k, :].bitcast(F32), ALU.subtract).then_inc(lo_done, 1)

            def ada_block(m, k, part, i=0):
                dve.wait_ge(ada_full[part], 16 * (DT * m + k - 1) + i * 32)
                if m < 3:
                    dve.wait_ge(ada_used, 3 * (DT * m + k) + part - 2 + i * 6)
                elif part < 2:
                    dve.wait_ge(ada_used, 9 * DT + 2 * k + part - 1 + i * 4)
                else:
                    dve.wait_ge(ada_used, 11 * DT + k + i * 2)
                if m == 1 and k == 0:
                    dve.tensor_scalar(ada_acc[:, part, :], ada_raw[part][:, :], c_silu[:, 0:1], None,
                                      ALU.mult).then_inc(ada_used, 1)
                else:
                    acc = sums_of[m][:, part, :]
                    dve.scalar_tensor_tensor(out=acc, in0=ada_raw[part][:, :],
                                             scalar=c_silu[:, bass.ds(i * 2 + k, 1)], in1=acc, op0=ALU.mult, op1=ALU.add
                                             ).then_inc(ada_used, 1)

            def ada_first(t):
                part, k = first_block(t)
                src = ada_raw[t % 3][:, :]
                if 3 <= t < 9:
                    src = early[t - 3]
                    dve.wait_ge(early_full[t - 3], 16)
                else:
                    dve.wait_ge(ada_full[t % 3], 16 if t < 3 else 16 * (t // 3 - 1))
                if k:
                    dve.wait_ge(ada_used, t - 1 if t < 2 * DT else t)
                if k == 0:
                    dve.tensor_scalar(ada_acc[:, part, :], src, c_silu[:, 0:1], None,
                                      ALU.mult).then_inc(ada_used, 1)
                else:
                    dve.scalar_tensor_tensor(out=ada_acc[:, part, :], in0=src,
                                             scalar=c_silu[:, k:k + 1], in1=ada_acc[:, part, :],
                                             op0=ALU.mult, op1=ALU.add).then_inc(ada_used, 1)

            def ada_next(m, count):
                for _ in range(count):
                    ada_block(m, ada_at[0] // 3, ada_at[0] % 3)
                    ada_at[0] += 1

            SCALE_SHIFT, GATE = slice(0, 2 * DT), slice(2 * DT, 3 * DT)

            def modulation(m, name=None, cols=SCALE_SHIFT):
                name = name or f"mod{m}"
                src = bank_full(dve, name)
                b = V_ADAB + 3 * DT * m
                bank_read(name, dve.tensor_tensor(MOD[:, m, cols], src[:, cols],
                                                  V[:, b + cols.start:b + cols.stop], ALU.add))
                bank_was_read(dve, name)
                if cols.start:
                    return
                dve.scalar_tensor_tensor(out=GAIN[:, m, :], in0=MOD[:, m, DT:2 * DT], scalar=1.0,
                                         in1=V[:, DT * m:DT * (m + 1)], op0=ALU.add, op1=ALU.mult
                                         ).then_inc(mod_ready, 1)
                dve.wait_ge(mod_ready, m + 1)

            ssq = [0]

            def add_squares(t, first):
                into = sq_sum if first else sq
                ins = dve.tensor_tensor(into[:, :, :], X[:, t:t + 2, :], X[:, t:t + 2, :], ALU.mult)
                if not first:
                    chain(ins)
                    ins = dve.tensor_tensor(sq_sum[:, :, :], sq_sum[:, :, :], sq[:, :, :], ALU.add)
                ins.then_inc(ssq_ready, 1)
                ssq[0] += 1
                dve.wait_ge(ssq_ready, ssq[0])

            def residual_pair(n, u, t, gate, squares=True):
                dve.wait_ge(block_used, n + 1)
                src = halves(G[u % 4])
                if gate is None:
                    ins = dve.tensor_tensor(X[:, t:t + 2, :], src, X[:, t:t + 2, :], ALU.add)
                else:
                    for m in range(2):
                        ins = dve.scalar_tensor_tensor(out=X[:, t + m, :], in0=src[:, m, :],
                                                       scalar=gate[:, t + m:t + m + 1], in1=X[:, t + m, :],
                                                       op0=ALU.mult, op1=ALU.add)
                ins.then_inc(g_free[u % 4], 1)
                if squares:
                    dve.wait_ge(g_free[u % 4], u // 4 + 1)
                    add_squares(t, t == 0)

            def clear_sums():
                dve.memset(sq_sum[:, 0, :], 0.0).then_inc(down_free0, 1)
                dve.memset(sq_sum[:, 1, :], 0.0).then_inc(down_free1, 1)

            def residual_tile(phase, n, g, m, gate, i=0):
                if m == 0:
                    dve.wait_ge(down_half, 4 * phase + g + 1 + i)
                else:
                    dve.wait_ge(block_used, n + 1 + i * 4)
                at = i * 2 + (2 * g + m)
                xt = X[:, bass.ds(at, 1), :].rearrange("p a s -> p (a s)")
                if gate is None:
                    ins = dve.tensor_tensor(xt, A[m][:, 0:S], xt, ALU.add)
                else:
                    ins = dve.scalar_tensor_tensor(out=xt, in0=A[m][:, 0:S], scalar=gate[:, bass.ds(at, 1)],
                                                   in1=xt, op0=ALU.mult, op1=ALU.add)
                free = (down_free0, down_free1)[m]
                ins.then_inc(free, 1)
                dve.wait_ge(free, 5 * phase + g + 2 + i)
                chain(dve.tensor_tensor(sq[:, m, :], xt, xt, ALU.mult))
                if phase == 1:
                    dve.scalar_tensor_tensor(out=HN[1][:, m, :], in0=sq[:, m, :],
                                             scalar=final_sq[:, bass.ds(at, 1)], in1=HN[1][:, m, :],
                                             op0=ALU.mult, op1=ALU.add)
                dve.tensor_tensor(sq_sum[:, m, :], sq_sum[:, m, :], sq[:, m, :], ALU.add
                                  ).then_inc(ssq_ready, 1)

            def low_pair(split, p, src, position=None, shift=None):
                position = p if position is None else position
                dve.wait_ge(hhi_ready, 4 * SPLIT[split] + position + 1)
                hi = h_hi[:, 2 * p:2 * p + 2, :].bitcast(F32)
                if shift is None:
                    ins = dve.tensor_tensor(h_lo[:, 2 * p:2 * p + 2, :], src, hi, ALU.subtract)
                else:
                    for m in range(2):
                        ins = dve.scalar_tensor_tensor(out=h_lo[:, 2 * p + m, :], in0=src[:, m, :],
                                                       scalar=shift[:, 2 * p + m:2 * p + m + 1],
                                                       in1=hi[:, m, :], op0=ALU.add, op1=ALU.subtract)
                ins.then_inc(h_ready, 1)

            def norm(split, k, gain, shift=None, roots=rstd):
                dve.wait_ge(rstd_ready, k + 1)
                for p in range(5):
                    if p < 4:
                        if p >= 2:
                            dve.wait_ge(h_ready, 4 * SPLIT[split] + p - 1)
                        for m in range(2):
                            t = 2 * p + m
                            ins = dve.scalar_tensor_tensor(out=HN[p % 2][:, m, :], in0=X[:, t, :],
                                                           scalar=gain[:, t:t + 1], in1=roots[:, :],
                                                           op0=ALU.mult, op1=ALU.mult)
                        ins.then_inc(norm_ready, 1)
                    if p >= 1:
                        dve.wait_ge(norm_ready, 4 * NORMED[split] + p)
                        low_pair(split, p - 1, HN[(p - 1) % 2][:, :, :], shift=shift)

            def norm_in_place(k, gain):
                dve.wait_ge(rstd_ready, k + 1)
                for t in range(DT):
                    ins = dve.scalar_tensor_tensor(out=X[:, t, :], in0=X[:, t, :], scalar=gain[:, t:t + 1],
                                                   in1=rstd[:, :], op0=ALU.mult, op1=ALU.mult)
                return ins

            def biased(r, v):
                hp, b = v // 2, v % 2
                keys = S if b else P
                src = halves(bank_full(dve, f"scores{r}{v}"))
                s = SS[:, v % 2, :, 0:keys]
                bank_read(f"scores{r}{v}",
                          dve.tensor_tensor(s, src[:, :, 0:keys],
                                            BIAS[:, 2 * hp:2 * hp + 2, S - keys:S], ALU.add))
                bank_was_read(dve, f"scores{r}{v}")
                mx, nm = stat[:, v % 2, 0:2], stat[:, v % 2, 2:4]
                chain(dve.tensor_reduce(mx, s, AX_X, ALU.max))
                if r == 0:
                    chain(dve.tensor_tensor(mx, mx, sinks[:, 2 * hp:2 * hp + 2], ALU.max))
                dve.tensor_scalar(nm, mx, -1.0, None, ALU.mult).then_inc(max_ready, 1)

            def scaled(r, v):
                keys = S if v % 2 else P
                dve.wait_ge(prob_ready, ATT_UNITS * r + v + 1)
                total, es = stat[:, v % 2, 4:6], stat[:, v % 2, 6:8]
                if r == 0:
                    chain(dve.tensor_tensor(total, total, es, ALU.add))
                chain(dve.reciprocal(total, total))
                for e in range(2):
                    pr = PR[:, v % 2, e, 0:keys]
                    ins = dve.tensor_scalar(pr, pr, total[:, e:e + 1], None, ALU.mult)
                ins.then_inc(prob_scaled, 1)

            def attended(r, v):
                t, b = v // 2 + (0 if r else 4), v % 2
                src = bank_full(dve, f"att_out{r}{v}")
                bank_read(f"att_out{r}{v}", dve.tensor_copy(MIX[:, t, b * P:b * P + P], src[:, 0:P]))

            def attention(r, v, n):
                if v < ATT_UNITS:
                    biased(r, v)
                split_lo(n)
                if v >= 2:
                    attended(r, v - 2)
                if v < ATT_UNITS:
                    scaled(r, v)

            dve.memset(ones[:, :], 1.0)
            dve.memset(eps6[:, :], EPS)
            dve.memset(eps5[:, :], GN_EPS)
            dve.memset(one[:, :], 1.0)
            dve.memset(reset[:, :], 1.0)
            dve.memset(ST[:, :, :, :], 0.0)
            dve.memset(t8[:, :], NEG).then_inc(setup_ready, 1)
            dve.wait_ge(setup_ready, 1)
            chain(dve.memset(reset[:, :].rearrange("p (c j) -> p c j", j=64)[:, :, 0:1], 0.0))
            src = bank_full(dve, "vecs")
            bank_read("vecs", dve.tensor_copy(V[:, :], src[:, 0:V_ALL]))
            src = bank_full(dve, "table")
            bank_read("table", dve.tensor_copy(t8[:, P:2 * P], src[0:HEADS, 0:P]))
            bank_was_read(dve, "vecs")
            dve.tensor_tensor(final_sq[:, :], V[:, V_FINAL:V_FINAL + DT], V[:, V_FINAL:V_FINAL + DT], ALU.mult)
            dve.wait_ge(c_sigmoid, 1)
            chain(dve.tensor_tensor(c_silu[:, :], c_tmp[:, :], V[:, V_C:V_C + DT], ALU.mult))
            for t in range(2 * DT):
                ada_first(t)
                if t % 2 and 3 <= t < 11:
                    q = (t - 3) // 2
                    bank_was_read(dve, f"x{q}")
                    add_squares(2 * q, q == 0)
            dve.wait_ge(g_split, 1)
            dve.tensor_tensor(g_lo[:, :, :], g_raw[:, :, :], g_hi[:, :, :].bitcast(F32), ALU.subtract
                              ).then_inc(g_ready, 1)
            split_lo(0)
            modulation(0)
            norm("n0", 0, GAIN[:, 0, :], MOD[:, 0, 0:DT])
            split_lo(1)

            split_lo(2)
            dve.wait_ge(block_used, 1)
            dve.tensor_copy(K4[:, 0, :], G[0][:, 0:S])
            dve.tensor_copy(K4[64:128, 1, :], G[0][0:64, 0:S])
            dve.tensor_copy(K4[0:64, 1, :], G[0][64:128, 0:S])
            dve.tensor_copy(V4[:, :, 0:P], G[0][:, S:2 * S].rearrange("p (k f) -> p k f", k=2)
                            ).then_inc(g_free[0], 1)
            for t in range(16, 19):
                ada_first(t)
            src = bank_full(dve, "glr")
            bank_read("glr", dve.tensor_copy(GLT[:, :, :], src[:, 0:32].rearrange("p (k r) -> p k r", k=2)))
            for q in range(4):
                bank_was_read(dve, f"flip{q}")
            dve.wait_ge(small_in, 48)
            attention(0, 0, 3)
            for t in range(19, 22):
                ada_first(t)
            src = bank_full(dve, "glt")
            bank_read("glt", dve.tensor_copy(GL[:, :], src[0:16, 0:S]))
            attention(0, 1, 4)
            for t in (22, 23):
                ada_first(t)
            attention(0, 2, 5)
            modulation(0, "gate0", GATE)
            ada_next(1, 2)
            attention(0, 3, 6)
            dve.wait_ge(z_ready, 1)
            chain(dve.scalar_tensor_tensor(out=GZ, in0=GZ, scalar=0.0, in1=GA, op0=ALU.min,
                                           op1=ALU.subtract))
            chain(dve.tensor_scalar(GZ, GZ, 1.0 / 16.0, None, ALU.mult))
            dve.tensor_tensor_scan(wide[:, 4, :], reset[:, :], wide[:, 2, :], 0.0, ALU.mult, ALU.add
                                   ).then_inc(decay_ready, 1)
            ada_next(1, 3)
            attention(0, 4, 7)
            ada_next(1, 3)
            attention(0, 5, 8)
            dve.wait_ge(exp_ready, 1)
            dve.tensor_tensor(GQ, GQ, EB, ALU.mult)
            dve.tensor_tensor(KE, GK, KE, ALU.mult)
            dve.tensor_tensor(GK, GK, ENB, ALU.mult).then_inc(gla_ready, 1)
            ada_next(1, 2)
            attention(0, 6, 9)
            bank_was_read(dve, "kend")
            chain(dve.memset(AM, 0.0))
            for k in range(2):
                src = bank_full(dve, f"gs{k}")
                bank_read(f"gs{k}", dve.copy_predicated(AM[:, k, :, :], spread(chunk_mask, 4),
                                                        src[:, :].rearrange("p (h s) -> p h s", h=4)))
            ada_next(1, 3)
            attention(0, 7, 10)
            def increments(name, at, m, ch):
                src = bank_full(dve, name)
                for e in range(2):
                    half = slice(64 * e, 64 * e + 64)
                    inc = src[half, at + e * P:at + e * P + P]
                    if ch == 0:
                        ins = dve.tensor_copy(ST[half, 2 * m + e, 0, :], inc)
                    else:
                        ins = dve.scalar_tensor_tensor(out=ST[half, 2 * m + e, ch, :],
                                                       in0=ST[half, 2 * m + e, ch - 1, :],
                                                       scalar=EB[half, m, ch * 64 + 63:ch * 64 + 64],
                                                       in1=inc, op0=ALU.mult, op1=ALU.add)
                return ins

            for m in range(2):
                chain(increments(f"ds{m}", 0, m, 0))
            for m in range(2):
                bank_read(f"ds{m}", increments(f"ds{m}", S, m, 1))
                bank_was_read(dve, f"ds{m}")
            attended(0, 6)
            increments("ds2", 0, 0, 2)
            bank_read("ds2", increments("ds2", S, 1, 2))
            attended(0, 7)
            ada_next(1, 4)
            for a, p in enumerate((2, 3)):
                low_pair("mix0", p, MIX[:, 2 * p:2 * p + 2, :], position=a)
            for m in range(2):
                dve.wait_ge(g_free[(3, 0)[m]], (2, 3)[m])
                chain(dve.tensor_tensor(GG[:, 2 * m:2 * m + 2, :], GG[:, 2 * m:2 * m + 2, :],
                                        GE[:, 2 * m:2 * m + 2, :], ALU.mult))
            for m in range(2):
                bank_was_read(dve, f"go{m}")
                o = O[:, 2 * m:2 * m + 2, :]
                dve.tensor_tensor(OSQ[:, 2 * m:2 * m + 2, :], o, o, ALU.mult).then_inc(osq_ready, 1)
            ada_next(1, 3)
            for m in range(2):
                dve.wait_ge(ors_ready, m + 1)
                mix = MIX[:, 2 * m:2 * m + 2, :]
                chain(dve.scalar_tensor_tensor(out=mix, in0=O[:, 2 * m:2 * m + 2, :],
                                               scalar=V[:, V_GLAW:V_GLAW + 1],
                                               in1=RO[:, 2 * m:2 * m + 2, :], op0=ALU.mult, op1=ALU.mult))
                dve.tensor_tensor(mix, mix, GG[:, 2 * m:2 * m + 2, :], ALU.mult).then_inc(mix_ready, 1)
                dve.wait_ge(mix_ready, m + 1)
            for m in range(2):
                low_pair("mix0", m, MIX[:, 2 * m:2 * m + 2, :], position=2 + m)
            for j in range(3):
                split_lo(N_OUT + j + 2)
                ada_next(1, (2, 1, 1)[j])
                residual_pair(N_OUT + j, 9 + j, 2 * j, MOD[:, 0, 2 * DT:])
            residual_pair(N_OUT + 3, 12, 6, MOD[:, 0, 2 * DT:])
            modulation(1)
            norm("n1", 1, GAIN[:, 1, :], MOD[:, 1, 0:DT])
            modulation(1, "gate1", GATE)
            split_lo(N_OUT + 5)

            def mlp(layer):
                with_ada = layer == 0
                clear_sums()
                if with_ada:
                    dve.wait_ge(acc_clear, 1)
                with dve.Fori(0, 4) as i:
                    done = 0
                    for j in range(4):
                        split_lo(N_UP[layer] + j + 2, i)
                        for _ in range((2, 1, 2, 1)[j] if with_ada else 0):
                            ada_block(2, done // 3, done % 3, i)
                            done += 1
                        if not with_ada and j % 2 == 0:
                            ada_block(3, j // 2, 2, i)
                        dve.wait_ge(uhi_ready, 16 * layer + j + 1 + i * 4)
                        at = bass.ds(i * 8 + 2 * j, 2)
                        dve.tensor_tensor(u_lo[:, at, :], relu[j % 2][:, :, :], u_hi[:, at, :].bitcast(F32),
                                          ALU.subtract).then_inc(u_ready, 1)
                if layer:
                    modulation(3, "gate3", GATE)
                    dve.wait_ge(u_ready, 32)
                    chain(dve.memset(HN[1][:, :, :], 0.0))
                start = chain.count
                with dve.Fori(0, 4) as i:
                    chain.looped = i * 2
                    done = 0
                    for j in range(4):
                        n = N_DOWN[layer] + j
                        if j < 3:
                            split_lo(n + 2, i)
                        for _ in range((2, 1, 1, 0)[j] if with_ada else 0):
                            ada_block(3, done // 2, done % 2, i)
                            done += 1
                    for m in range(2):
                        residual_tile(layer, n, 0, m, MOD[:, 1 + 2 * layer, 2 * DT:], i)
                    split_lo(n + 2, i)
                chain.looped, chain.count = 0, start + 8
                ssq[0] += 8

            mlp(0)

            modulation(2)
            dve.wait_ge(rstd_ready, 3)
            for buf in (*pad, win):
                ins = dve.memset(buf[:, :, 0:POOL_PAD], 0.0)
            H = pad[0]
            for t in range(DT):
                ins = dve.scalar_tensor_tensor(out=H[:, t, POOL_PAD:], in0=X[:, t, :],
                                               scalar=GAIN[:, 2, t:t + 1], in1=rstd[:, :],
                                               op0=ALU.mult, op1=ALU.mult)
                if t % 2:
                    ins.then_inc(pool_normed, 1)
            for g in range(5):
                if g < 4:
                    tiles = slice(2 * g, 2 * g + 2)
                    dve.wait_ge(pool_shifted, g + 1)
                    src = H
                    for n in range(g + 1):
                        back = 1 << n
                        into = (pad[1], win)[n % 2]
                        chain(dve.tensor_tensor(into[:, tiles, POOL_PAD:], src[:, tiles, POOL_PAD:],
                                                src[:, tiles, POOL_PAD - back:POOL_PAD + S - back], ALU.add))
                        src = into
                    if g >= 2:
                        dve.wait_ge(h_ready, 4 * SPLIT["pool"] + g - 1)
                    hn, head = HN[g % 2], src[:, tiles, POOL_PAD:2 * POOL_PAD]
                    count = spread(C[:, C_CNT_AT + g * POOL_PAD:C_CNT_AT + (g + 1) * POOL_PAD], 2)
                    chain(dve.tensor_tensor(head, head, count, ALU.mult))
                    dve.scalar_tensor_tensor(out=hn[:, :, POOL_PAD:], in0=src[:, tiles, 2 * POOL_PAD:],
                                             scalar=1.0 / (2 << g), in1=H[:, tiles, 2 * POOL_PAD:],
                                             op0=ALU.mult, op1=ALU.subtract)
                    dve.tensor_tensor(hn[:, :, 0:POOL_PAD], head, H[:, tiles, POOL_PAD:2 * POOL_PAD],
                                      ALU.subtract).then_inc(norm_ready, 1)
                if g >= 1:
                    dve.wait_ge(norm_ready, 4 * NORMED["pool"] + g)
                    low_pair("pool", g - 1, HN[(g - 1) % 2][:, :, :])
            modulation(2, "gate2", GATE)
            chain(dve.tensor_tensor(gate_ps[:, :], MOD[:, 2, 2 * DT:], V[:, V_PSCALE:V_PSCALE + DT], ALU.mult))
            for g in range(4):
                residual_pair(N_POOL, U_POOL + g, 2 * g, gate_ps, squares=False)
            modulation(3)
            norm("n3", 3, GAIN[:, 3, :], MOD[:, 3, 0:DT])
            split_lo(N_POOL + 2)
            mlp(1)
            src = bank_full(dve, "ms5")
            dve.wait_ge(rstd_ready, 5)
            bank_read("ms5", dve.tensor_tensor(ln_ms5[:, :], src[:, 0:S], rstd[:, :], ALU.mult))
            bank_was_read(dve, "ms5")
            dve.tensor_tensor(ln_ms5[:, :], ln_ms5[:, :], rstd[:, :], ALU.mult).then_inc(ms5_scaled, 1)
            chain(norm_in_place(4, V[:, V_FINAL:V_FINAL + DT]))
            norm("n5", 5, V[:, V_ATTN2:V_ATTN2 + DT], roots=rstd5)

            for h in range(HEADS):
                ins = dve.tensor_scalar(BIAS[:, h, :], C[:, C_DIST:C_DIST + S], 2.0 ** -(h + 1), None,
                                        ALU.mult)
            chain(ins)
            for j in range(3):
                split_lo(N_IN2 + j + 2)
            for j in range(3, 13):
                attention(1, j - 3, N_IN2 + j + 2)
            dve.wait_ge(decay_in, 16)
            for h in range(4):
                if h == 2:
                    split_lo(N_IN2 + 15)
                src = bank_full(dve, f"rs{h}")
                dve.tensor_tensor(RS[h][:, 0:S], src[:, 0:S], DECAY[:, h, :], ALU.mult)
                bank_read(f"rs{h}", dve.tensor_tensor(RS[h][:, S:S + P], src[:, S:S + P], DECAY[:, h, 0:P],
                                                      ALU.mult))
            for p in range(2):
                low_pair("mix1", p, MIX[:, 2 * p:2 * p + 2, :])
            for m in range(2):
                u = U_IN2 + 12 + m
                dve.wait_ge(g_free[u % 4], u // 4 + 1)
                chain(dve.tensor_tensor(RG[:, 2 * m:2 * m + 2, :], RG[:, 2 * m:2 * m + 2, :],
                                        RT[:, 2 * m:2 * m + 2, :], ALU.mult))
            for m in range(2):
                src = bank_full(dve, f"rm{m}")
                o = GG[:, 2 * m:2 * m + 2, :]
                bank_read(f"rm{m}", dve.scalar_tensor_tensor(out=o, in0=halves(src), scalar=-1.0 / P, in1=o,
                                                             op0=ALU.mult, op1=ALU.add))
                bank_was_read(dve, f"rm{m}")
                dve.tensor_tensor(OSQ[:, 2 * m:2 * m + 2, :], o, o, ALU.mult).then_inc(osq_ready, 1)
            for m in range(2):
                dve.wait_ge(ors_ready, 2 + m + 1)
                mix = MIX[:, 4 + 2 * m:6 + 2 * m, :]
                for e in range(2):
                    h = 2 * m + e
                    ins = dve.scalar_tensor_tensor(out=MIX[:, 4 + h, :], in0=GG[:, h, :],
                                                   scalar=V[:, V_RET + h:V_RET + h + 1], in1=RO[:, h, :],
                                                   op0=ALU.mult, op1=ALU.mult)
                chain(ins)
                dve.tensor_tensor(mix, mix, RG[:, 2 * m:2 * m + 2, :], ALU.mult).then_inc(mix_ready, 1)
                dve.wait_ge(mix_ready, 2 + m + 1)
            for m in range(2):
                low_pair("mix1", 2 + m, MIX[:, 4 + 2 * m:6 + 2 * m, :])
            for j in range(3):
                split_lo(N_OUT2 + j + 2)
                residual_pair(N_OUT2 + j, U_OUT2 + j, 2 * j, None)
            residual_pair(N_OUT2 + 3, U_OUT2 + 3, 6, None)
            norm("n6", 6, V[:, V_FFN2:V_FFN2 + DT])
            clear_sums()
            dve.memset(UP[:, :, 0:2], 0.0).then_inc(pads_ready, 1)
            split_lo(N_OUT2 + 5)

            def gated_up(j, i=0):
                u = U_FFN + j
                dve.wait_ge(g_free[u % 4], u // 4 + 1 + i)
                def vec(base, m):
                    return V[:, bass.ds(i * 4 + (base + 2 * (j // 2) + m), 1)] if j < 20 else \
                        V[:, base + 20 + m:base + 21 + m]
                for m in range(2):
                    ins = dve.tensor_scalar(CV[:, m, :], UP[:, m, 2:], vec(V_CONVW + 2 * F2T, m),
                                            vec(V_CONVB, m), ALU.mult, ALU.add)
                chain(ins)
                for tap in (1, 0):
                    for m in range(2):
                        ins = dve.scalar_tensor_tensor(out=CV[:, m, :], in0=UP[:, m, tap:tap + S],
                                                       scalar=vec(V_CONVW + tap * F2T, m), in1=CV[:, m, :],
                                                       op0=ALU.mult, op1=ALU.add)
                    if tap:
                        chain(ins)
                ins.then_inc(conv_ready, 1)

            def gated_gate(j, i=0):
                u, p = U_FFN + j, j // 2
                dve.wait_ge(gelu_ready, p + 1 + i * 2)
                dve.wait_ge(block_used, N_FFN + j + 1 + i * 4)
                dve.tensor_tensor(GU[:, :, :], halves(G[u % 4]), GU[:, :, :], ALU.mult
                                  ).then_inc(g_free[u % 4], 1)
                dve.wait_ge(fhi_ready, p + 1 + i * 2)
                at = bass.ds(i * 4 + 2 * p, 2) if j < 20 else slice(20, 22)
                dve.tensor_tensor(f_lo[:, at, :], GU[:, :, :], f_hi[:, at, :].bitcast(F32), ALU.subtract
                                  ).then_inc(f_ready, 1)

            start = chain.count
            with dve.Fori(0, 5) as i:
                chain.looped = i * 4
                for j in range(4):
                    split_lo(N_FFN + j + 2, i)
                    (gated_gate if j % 2 else gated_up)(j, i)
            chain.looped, chain.count = 0, start + 20
            for j in (20, 21):
                split_lo(N_FFN + j + 2)
                (gated_gate if j % 2 else gated_up)(j)
            for g in range(4):
                for j in range(3):
                    if j < 2:
                        split_lo(N_FDOWN + 3 * g + j + 2)
                for m in range(2):
                    residual_tile(2, N_FDOWN + 3 * g + 2, g, m, None)
                    ssq[0] += 1
                split_lo(N_FDOWN + 3 * g + 4)
                if g == 0:
                    dve.wait_ge(phi_ready, 1)
                    dve.tensor_tensor(p_lo[:, :, :], p_t[:, :, :], p_hi[:, :, :].bitcast(F32), ALU.subtract
                                      ).then_inc(p_ready, 1)
            norm("n7", 7, V[:, V_PLE2:V_PLE2 + DT])
            split_lo(N_PLE + 2)
            for j in range(4):
                if j < 2:
                    split_lo(N_PLEG + j + 2)
                u = U_PLEG + j
                dve.wait_ge(g_free[u % 4], u // 4 + 1)
                chain(dve.tensor_tensor(SG[:, :, :], SG[:, :, :], PE8[:, 2 * j:2 * j + 2, :], ALU.mult))
                chain(dve.tensor_tensor(X[:, 2 * j:2 * j + 2, :], X[:, 2 * j:2 * j + 2, :], SG[:, :, :],
                                        ALU.add))
                add_squares(2 * j, j == 0)
                for t in (2 * j, 2 * j + 1):
                    ins = dve.tensor_scalar(X[:, t, :], X[:, t, :], V[:, V_FINAL2 + t:V_FINAL2 + t + 1], None,
                                            ALU.mult)
                ins.then_inc(fin_ready, 1)
            dve.wait_ge(token_rstd, 1)
            for k in range(2):
                for q in (2, 3):
                    src = bank_full(dve, f"out{q}")
                    ins = dve.tensor_scalar(orow[:, k, 2 * q * P:2 * (q + 1) * P], halves(src)[:, k, :],
                                            t_rstd[:, k:k + 1], None, ALU.mult)
                ins.then_inc(rows_dve, 1)

        @block.scalar
        def _(act):
            chain = Chain(act, act_step)

            def split_hi(n, i=0):
                k = k_tiles(n)
                act.wait_ge(raw_full[n % RAW], 16 * (n // RAW + 1) + i * 16)
                if n >= 2:
                    act.wait_ge(block_used, n - 1 + i * 4)
                act.activation(w_hi[n % 2][:, 0:k, :], raw[n % RAW][:, 0:k, :], ACT.Copy
                               ).then_inc(hi_done, 1)

            def preload_ln():
                chain(act.activation(unused[:, :], eps6[:, :], ACT.Ln))

            def root(norm):
                preload_ln()
                src = bank_full(act, f"ms{norm}")
                bank_read(f"ms{norm}", act.activation(ln_ms[:, :], src[:, 0:S], ACT.Ln, bias=eps6[:, 0:1],
                                                      scale=1.0 / D))
                bank_was_read(act, f"ms{norm}")
                act.activation(rstd[:, :], ln_ms[:, :], ACT.Exp, scale=-0.5).then_inc(rstd_ready, 1)

            def high_norm(split, shift=None):
                for p in range(4):
                    act.wait_ge(norm_ready, 4 * NORMED[split] + p + 1)
                    src = HN[p % 2]
                    if shift is None:
                        ins = act.activation(h_hi[:, 2 * p:2 * p + 2, :], src[:, :, :], ACT.Copy)
                    else:
                        for m in range(2):
                            t = 2 * p + m
                            ins = act.activation(h_hi[:, t, :], src[:, m, :], ACT.Identity,
                                                 bias=shift[:, t:t + 1])
                    ins.then_inc(hhi_ready, 1)

            def high_mix(p):
                act.activation(h_hi[:, 2 * p:2 * p + 2, :], MIX[:, 2 * p:2 * p + 2, :], ACT.Copy
                               ).then_inc(hhi_ready, 1)

            def leave(n, u, dst, scale=1.0):
                act.wait_ge(block_used, n + 1)
                act.activation(dst, halves(G[u % 4]), ACT.Copy, scale=scale).then_inc(g_free[u % 4], 1)

            def silu_parts(n, u, sigmoid, plain):
                act.wait_ge(block_used, n + 1)
                act.activation(plain, halves(G[u % 4]), ACT.Copy)
                act.activation(sigmoid, halves(G[u % 4]), ACT.Sigmoid).then_inc(g_free[u % 4], 1)

            def attention(r, v):
                if 1 <= v <= ATT_UNITS:
                    w = v - 1
                    src = bank_full(act, f"turned{r}{w}")
                    dst = PT[:, w % 2, :, :].rearrange("p (e k) s -> p e k s", e=2)[:, :, 0:w % 2 + 1, :]
                    bank_read(f"turned{r}{w}", act.activation(
                        dst, src[:, :].rearrange("p (e k s) -> p e k s", e=2, k=2)[:, :, 0:w % 2 + 1, :],
                        ACT.Copy))
                if v < ATT_UNITS:
                    hp, keys = v // 2, S if v % 2 else P
                    act.wait_ge(max_ready, ATT_UNITS * r + v + 1)
                    for e in range(2):
                        nm = stat[:, v % 2, 2 + e:3 + e]
                        if r == 0:
                            h = 2 * hp + e
                            act.activation(stat[:, v % 2, 6 + e:7 + e], sinks[:, h:h + 1], ACT.Exp, bias=nm)
                        ins = act.activation(PR[:, v % 2, e, 0:keys], SS[:, v % 2, e, 0:keys], ACT.Exp,
                                             bias=nm, accum_out=stat[:, v % 2, 4 + e:5 + e])
                    ins.then_inc(prob_ready, 1)

            def head_roots(names, eps):
                preload_ln()
                for m, name in enumerate(names):
                    src = bank_full(act, name)
                    bank_read(name, act.activation(RO[:, 2 * m:2 * m + 2, :], halves(src), ACT.Ln,
                                                   bias=eps[:, 0:1], scale=1.0 / P))
                for m, name in enumerate(names):
                    bank_was_read(act, name)
                    act.activation(RO[:, 2 * m:2 * m + 2, :], RO[:, 2 * m:2 * m + 2, :], ACT.Exp, scale=-0.5
                                   ).then_inc(ors_ready, 1)

            bank_was_read(act, "vecs")
            act.activation(c_tmp[:, :], V[:, V_C:V_C + DT], ACT.Sigmoid).then_inc(c_sigmoid, 1)
            for q in range(4):
                src = bank_full(act, f"x{q}")
                bank_read(f"x{q}", act.activation(X[:, 2 * q:2 * q + 2, :], halves(src), ACT.Copy))
            act.wait_ge(glr_in, 16)
            act.activation(g_hi[:, :, :], g_raw[:, :, :], ACT.Copy).then_inc(g_split, 1)
            for q in range(4):
                src = bank_full(act, f"flip{q}")
                bank_read(f"flip{q}", act.activation(BIAS[:, 2 * q:2 * q + 2, :], halves(src), ACT.Copy))
            split_hi(0)
            root(0)
            act.wait_ge(mod_ready, 1)
            high_norm("n0", MOD[:, 0, 0:DT])
            split_hi(1)

            split_hi(2)
            leave(1, 1, Q4[:, 0:2, :], 0.125)
            split_hi(3)
            attention(0, 0)
            leave(2, 2, Q4[:, 2:4, :], 0.125)
            split_hi(4)
            attention(0, 1)
            leave(3, 3, GQ, 0.125)
            split_hi(5)
            src = bank_full(act, "logits")
            for m in range(2):
                act.activation(GZ[:, m, :], halves(src)[:, m, :], ACT.Identity,
                               bias=V[:, V_BGATE + m:V_BGATE + m + 1])
            for m in range(2):
                ins = act.activation(GA[:, m, :], halves(src)[:, m, :], ACT.Abs,
                                     bias=V[:, V_BGATE + m:V_BGATE + m + 1])
            bank_read("logits", ins)
            attention(0, 2)
            bank_was_read(act, "logits")
            chain(act.activation(GA, GA, ACT.Exp, scale=-1.0))
            act.activation(GA, GA, ACT.Ln, bias=one[:, 0:1]).then_inc(z_ready, 1)
            leave(4, 4, GK)
            split_hi(6)
            attention(0, 3)
            leave(5, 5, GV[:, :, 0:S])
            split_hi(7)
            attention(0, 4)
            act.wait_ge(decay_ready, 1)
            act.activation(EB, GB, ACT.Exp)
            act.activation(ENB, GB, ACT.Exp, scale=-1.0)
            for m in range(2):
                for ch in range(4):
                    toks = slice(ch * 64, ch * 64 + 64)
                    ins = act.activation(KE[:, m, toks], GB[:, m, toks], ACT.Exp, scale=-1.0,
                                         bias=GB[:, m, ch * 64 + 63:ch * 64 + 64])
            ins.then_inc(exp_ready, 1)
            leave(6, 6, GV[:, :, S:2 * S])
            split_hi(8)
            attention(0, 5)
            act.wait_ge(block_used, 8)
            split_hi(9)
            src = bank_full(act, "kend")
            bank_read("kend", act.activation(KET, src[:, :].rearrange("p (a s) -> p a s", a=4), ACT.Copy))
            attention(0, 6)
            split_hi(10)
            attention(0, 7)
            silu_parts(7, 7, GE[:, 0:2, :], GG[:, 0:2, :])
            silu_parts(8, 8, GE[:, 2:4, :], GG[:, 2:4, :])
            attention(0, 8)
            bank_was_read(act, "att_out07")
            for p in (2, 3):
                high_mix(p)
            for m in range(2):
                src = bank_full(act, f"go{m}")
                bank_read(f"go{m}", act.activation(O[:, 2 * m:2 * m + 2, :], halves(src), ACT.Copy))
            head_roots(("gm0", "gm1"), eps6)
            for m in range(2):
                act.wait_ge(mix_ready, m + 1)
                high_mix(m)
            for j in range(4):
                split_hi(N_OUT + j + 2)
            root(1)
            act.wait_ge(mod_ready, 2)
            high_norm("n1", MOD[:, 1, 0:DT])

            def mlp(layer):
                start = chain.count
                with act.Fori(0, 4) as i:
                    chain.looped = i * 4
                    for j in range(4):
                        n, u = N_UP[layer] + j, U_UP[layer] + j
                        split_hi(n + 2, i)
                        act.wait_ge(block_used, n + 1 + i * 4)
                        act.wait_ge(lo_done, n + 2 + i * 4)
                        act.activation(relu[j % 2][:, :, :], halves(G[u % 4]), ACT.Relu
                                       ).then_inc(g_free[u % 4], 1)
                        act.wait_ge(g_free[u % 4], u // 4 + 1 + i)
                        chain(act.activation(relu[j % 2][:, :, :], relu[j % 2][:, :, :], ACT.Square))
                        act.activation(u_hi[:, bass.ds(i * 8 + 2 * j, 2), :], relu[j % 2][:, :, :],
                                       ACT.Copy).then_inc(uhi_ready, 1)
                chain.looped, chain.count = 0, start + 16
                with act.Fori(0, 4) as i:
                    for j in range(4):
                        split_hi(N_DOWN[layer] + j + 2, i)

            mlp(0)
            root(2)
            for g in range(4):
                act.wait_ge(pool_normed, g + 1)
                for t in (2 * g, 2 * g + 1):
                    ins = act.activation(pad[0][:, t, POOL_PAD:], pad[0][:, t, POOL_PAD:], ACT.Identity,
                                         bias=MOD[:, 2, t:t + 1])
                ins.then_inc(pool_shifted, 1)
            for g in range(4):
                act.wait_ge(norm_ready, 4 * NORMED["pool"] + g + 1)
                act.activation(h_hi[:, 2 * g:2 * g + 2, :], HN[g % 2][:, :, :], ACT.Copy
                               ).then_inc(hhi_ready, 1)
            for g in range(4):
                u = U_POOL + g
                act.wait_ge(g_free[u % 4], u // 4 + 1)
                act.activation(pool_squares[g][:, :, :], X[:, 2 * g:2 * g + 2, :], ACT.Square
                               ).then_inc(pool_squared, 1)
            root(3)
            act.wait_ge(mod_ready, 4)
            high_norm("n3", MOD[:, 3, 0:DT])
            split_hi(N_POOL + 2)
            mlp(1)
            root(4)
            preload_ln()
            act.wait_ge(ms5_scaled, 1)
            chain(act.activation(ln_ms5[:, :], ln_ms5[:, :], ACT.Ln, bias=eps6[:, 0:1], scale=1.0 / D))
            act.activation(rstd5[:, :], ln_ms5[:, :], ACT.Exp, scale=-0.5).then_inc(rstd_ready, 1)
            high_norm("n5")

            outs = [(Q4[:, 0:2, :], 0.125), (Q4[:, 2:4, :], 0.125), (K4[:, 0:2, :], 1.0),
                    (K4[:, 2:4, :], 1.0), (V4[:, :, 0:S], 1.0), (V4[:, :, S:2 * S], 1.0),
                    (RQ[:, 0:2, :], 1.0), (RQ[:, 2:4, :], 1.0), (RK[:, 0:2, :], 128 ** -0.5),
                    (RK[:, 2:4, :], 128 ** -0.5), (V4r[:, :, 0:S], 1.0), (V4r[:, :, S:2 * S], 1.0)]
            for j in range(14):
                if j < 12:
                    leave(N_IN2 + j, U_IN2 + j, *outs[j])
                split_hi(N_IN2 + j + 2)
                if j >= 12:
                    a = 2 * (j - 12)
                    silu_parts(N_IN2 + j, U_IN2 + j, RT[:, a:a + 2, :], RG[:, a:a + 2, :])
                if 3 <= j < 12:
                    attention(1, j - 3)
            bank_was_read(act, "att_out17")
            for p in range(2):
                high_mix(p)
            for m in range(2):
                src = bank_full(act, f"ro{m}")
                bank_read(f"ro{m}", act.activation(GG[:, 2 * m:2 * m + 2, :], halves(src), ACT.Copy))
            head_roots(("rv0", "rv1"), eps5)
            for m in range(2):
                act.wait_ge(mix_ready, 2 + m + 1)
                high_mix(2 + m)
            for j in range(4):
                split_hi(N_OUT2 + j + 2)
            root(6)
            high_norm("n6")

            def gated_up(j, i=0):
                u, p = U_FFN + j, j // 2
                act.wait_ge(block_used, N_FFN + j + 1 + i * 4)
                act.activation(UP[:, :, 2:], halves(G[u % 4]), ACT.Copy).then_inc(g_free[u % 4], 1)

            def gated_gate(j, i=0):
                u, p = U_FFN + j, j // 2
                act.wait_ge(conv_ready, p + 1 + i * 2)
                act.activation(GU[:, :, :], CV[:, :, :], ACT.Gelu_apprx_tanh).then_inc(gelu_ready, 1)
                act.wait_ge(g_free[u % 4], u // 4 + 1 + i)
                at = bass.ds(i * 4 + 2 * p, 2) if j < 20 else slice(20, 22)
                act.activation(f_hi[:, at, :], GU[:, :, :], ACT.Copy).then_inc(fhi_ready, 1)

            act.wait_ge(pads_ready, 1)
            with act.Fori(0, 5) as i:
                for j in range(4):
                    split_hi(N_FFN + j + 2, i)
                    if j % 2:
                        gated_gate(j, i)
                    else:
                        gated_up(j, i)
            split_hi(N_FFN + 22)
            gated_up(20)
            split_hi(N_FFN + 23)
            gated_gate(21)
            for g in range(4):
                for j in range(3):
                    split_hi(N_FDOWN + 3 * g + j + 2)
                if g == 0:
                    src = bank_full(act, "pt")
                    bank_read("pt", act.activation(p_t[:, :, :], halves(src), ACT.Copy))
                    bank_was_read(act, "pt")
                    act.activation(p_hi[:, :, :], p_t[:, :, :], ACT.Copy).then_inc(phi_ready, 1)
            root(7)
            high_norm("n7")
            split_hi(N_PLE + 2)
            for g in range(4):
                leave(N_PLE, U_PLE + g, PE8[:, 2 * g:2 * g + 2, :])
            for j in range(4):
                if j < 2:
                    split_hi(N_PLEG + j + 2)
                u = U_PLEG + j
                act.wait_ge(block_used, N_PLEG + j + 1)
                if j:
                    act.wait_ge(ssq_ready, SQUARES[7] + j)
                act.activation(SG[:, :, :], halves(G[u % 4]), ACT.Sigmoid).then_inc(g_free[u % 4], 1)
            preload_ln()
            act.wait_ge(token_ms, 1)
            chain(act.activation(t_ln[:, :], G[(U_PLEG + 4) % 4][:, 0:2], ACT.Ln, bias=eps6[:, 0:1],
                                 scale=1.0 / D))
            act.activation(t_rstd[:, :], t_ln[:, :], ACT.Exp, scale=-0.5).then_inc(token_rstd, 1)
            act.wait_ge(token_rstd, 1)
            for k in range(2):
                for q in (0, 1):
                    src = bank_full(act, f"out{q}")
                    ins = act.activation(orow[:, k, 2 * q * P:2 * (q + 1) * P], halves(src)[:, k, :],
                                         ACT.Identity, scale=t_rstd[:, k:k + 1])
                ins.then_inc(rows_act, 1)


_INS = ['x', 'c', 'norm_w', 'ada_w', 'ada_b', 'attn_w_in', 'gla_w_gate', 'gla_b_gate', 'gla_norm_w',
        'attn_sinks', 'attn_w_out', 'rel_bias', 'pool_w', 'pool_scale', 'mlp_w1', 'mlp_w2', 'final_norm_w',
        'p_2', 'attn_norm_2', 'w_in_2', 'ret_norm_2', 'w_out_2', 'ffn_norm_2', 'w_up_2', 'w_gate_2',
        'conv_w_2', 'conv_b_2', 'w_down_2', 'ple_norm_2', 'w_ple_2', 'w_ple_gate_2', 'final_norm_2']
_OUTS = [((1, 256, 1024), 'float32')]


def shape_constants():
    import numpy as np

    out = np.zeros((P, C_ALL), np.float32)
    p, f = np.arange(P)[:, None], np.arange(P)[None, :]
    out[:, C_ID:C_ID + P] = p == f
    out[:, C_ANTI:C_ANTI + P] = p + f == P - 1
    dist = np.arange(P)[::-1]
    d = np.maximum(dist, 1).astype(np.float64)
    large = np.minimum(16 + (np.log(d / 16) / np.log(128 / 16) * 16).astype(np.int32), 31)
    bucket = np.where(dist < 16, dist, large)
    out[0:32, C_HOT:C_HOT + P] = np.arange(32)[:, None] == bucket[None, :]
    out[:, C_MASK:C_MASK + P] = (p // 64 == f // 64) & (p <= f)
    gap = (P + p - np.arange(S)[None, :]).astype(np.float32)
    out[:, C_DIST:C_DIST + S] = np.where(gap >= 0, -gap, np.float32(NEG))
    diff = np.arange(S)[None, :] - p
    for h in range(4):
        log_g = np.log(np.float32(1.0) - np.exp2(np.float32(-5.0 - h)), dtype=np.float32)
        decay = np.where(diff >= 0, np.exp(log_g * np.maximum(diff, 0).astype(np.float32)), 0.0)
        out[:, C_DECAY + h * S:C_DECAY + (h + 1) * S] = decay
    for g in range(4):
        out[:, C_CNT + g * POOL_PAD:C_CNT + (g + 1) * POOL_PAD] = \
            np.float32(1.0) / np.minimum(np.arange(POOL_PAD) + 1, 2 << g).astype(np.float32)
    return out


def kernel(**inputs):
    import numpy as _np
    import concourse.bacc as _bacc
    from concourse import mybir as _mybir
    from concourse.bass_utils import run_bass_kernel_spmd as _run

    nc = _bacc.Bacc("TRN2", target_bir_lowering=False, num_devices=1)
    arrays, args = {}, []
    for name in [*_INS, "shape_consts"]:
        a = _np.ascontiguousarray(inputs[name]) if name in inputs else shape_constants()
        arrays[f"in_{name}_dram"] = a
        args.append(nc.dram_tensor(f"in_{name}_dram", a.shape, _mybir.dt.from_np(a.dtype), kind="ExternalInput").ap())
    for i, (shape, dtype) in enumerate(_OUTS):
        dt = _mybir.dt.from_np(_np.dtype(dtype))
        args.append(nc.dram_tensor(f"out_{i}_dram", shape, dt, kind="ExternalOutput").ap())
    build(nc, *args)
    r = _run(nc, [arrays], core_ids=[0])
    got = tuple(r.results[0][f"out_{i}_dram"] for i in range(len(_OUTS)))
    return got[0]
```
